# Optimizing a Trainium2 kernel written in Bass

```python
import math
import jax, jax.numpy as jnp
from jax import lax
import numpy as np

D_MODEL = 1024
BATCH = 1
SEQ = 512
DEPTH = 2

D_BRANCH = 512
M_HEADS = 4
M_HEAD_DIM = D_BRANCH // M_HEADS
M_CHUNK = 64
M_CONV = 4
R_BLOCKS = 8
R_BLOCK_DIM = D_BRANCH // R_BLOCKS
R_CONV = 4
R_C = 8.0
A_HEADS = 8
A_HEAD_DIM = D_BRANCH // A_HEADS
IDX_HEADS = 8
IDX_DIM = 64
TOPK_MAX = 256
Q_BLOCK = 128
ROPE_THETA = 10000.0
D_FF = 3 * D_MODEL
FFN_CONV = 3
EPS = 1e-6

IN_SPLITS = (
    2 * D_BRANCH,
    D_BRANCH,
    D_BRANCH,
    M_HEADS,
    M_HEADS,
    D_BRANCH,
    D_BRANCH,
    D_BRANCH,
    D_BRANCH,
    D_BRANCH,
    IDX_HEADS * IDX_DIM,
    IDX_DIM,
    IDX_HEADS,
    3 * D_MODEL,
)
N_IN = sum(IN_SPLITS)


def rms_norm(x, g):
    xf = x.astype(jnp.float32)
    y = xf * lax.rsqrt(jnp.mean(xf * xf, axis=-1, keepdims=True) + EPS)
    return (y * g.astype(jnp.float32)).astype(x.dtype)

def causal_dwconv(x, w, b):
    K, C = w.shape
    y = lax.conv_general_dilated(x, w[:, None, :].astype(x.dtype), window_strides=(1,),
                                 padding=[(K - 1, 0)], dimension_numbers=('NWC', 'WIO', 'NWC'),
                                 feature_group_count=C)
    return y + b.astype(x.dtype)

def rope_tables(positions, dim):
    inv = ROPE_THETA ** (-jnp.arange(0, dim, 2, dtype=jnp.float32) / dim)
    ang = positions.astype(jnp.float32)[..., None] * inv
    return jnp.cos(ang), jnp.sin(ang)

def apply_rope(x, cos, sin):
    x1, x2 = jnp.split(x.astype(jnp.float32), 2, axis=-1)
    c = cos[:, :, None, :]
    s = sin[:, :, None, :]
    return jnp.concatenate([x1 * c - x2 * s, x2 * c + x1 * s], axis=-1).astype(x.dtype)

def head_layer_norm(h, g):
    B, S, H, Dh = h.shape
    mu = jnp.mean(h, axis=-1, keepdims=True)
    var = jnp.mean(jnp.square(h - mu), axis=-1, keepdims=True)
    y = (h - mu) * lax.rsqrt(var + EPS)
    return y.reshape(B, S, H * Dh) * g.astype(jnp.float32)

def mlstm_chunkwise(q, k, v, i_pre, f_pre):
    B, S, H, Dh = q.shape
    L = M_CHUNK
    nc = S // L
    f32 = jnp.float32

    def to_chunks(t):
        return t.astype(f32).reshape(B, nc, L, H, Dh).transpose(1, 0, 3, 2, 4)

    def gate_chunks(t):
        return t.astype(f32).reshape(B, nc, L, H).transpose(1, 0, 3, 2)

    qc = to_chunks(q)
    kc = to_chunks(k) * (Dh ** -0.5)
    vc = to_chunks(v)
    ic = gate_chunks(i_pre)
    gc = jnp.cumsum(jax.nn.log_sigmoid(gate_chunks(f_pre)), axis=-1)
    causal = jnp.tril(jnp.ones((L, L), dtype=bool))

    def step(carry, inp):
        C, n, m = carry
        qb, kb, vb, ib, gb = inp
        logd = jnp.where(causal, gb[..., :, None] - gb[..., None, :] + ib[..., None, :], -jnp.inf)
        log_inter = gb + m[..., None]
        m_t = jnp.maximum(log_inter, jnp.max(logd, axis=-1))
        s = jnp.einsum('bhtd,bhsd->bhts', qb, kb) * jnp.exp(logd - m_t[..., None])
        w_inter = jnp.exp(log_inter - m_t)
        num = jnp.einsum('bhts,bhsd->bhtd', s, vb) + w_inter[..., None] * jnp.einsum('bhvk,bhtk->bhtv', C, qb)
        den = jnp.sum(s, axis=-1) + w_inter * jnp.einsum('bhk,bhtk->bht', n, qb)
        h = num / jnp.maximum(jnp.abs(den), jnp.exp(-m_t))[..., None]
        g_last = gb[..., -1]
        m_new = m_t[..., -1]
        w_state = jnp.exp(g_last[..., None] - gb + ib - m_new[..., None])
        decay = jnp.exp(g_last + m - m_new)
        C = decay[..., None, None] * C + jnp.einsum('bhs,bhsv,bhsk->bhvk', w_state, vb, kb)
        n = decay[..., None] * n + jnp.einsum('bhs,bhsk->bhk', w_state, kb)
        return (C, n, m_new), h

    init = (jnp.zeros((B, H, Dh, Dh), f32), jnp.zeros((B, H, Dh), f32), jnp.zeros((B, H), f32))
    _, hs = lax.scan(step, init, (qc, kc, vc, ic, gc))
    return hs.transpose(1, 0, 3, 2, 4).reshape(B, S, H, Dh)

def rg_lru(x, w_a, b_a, w_x, b_x, lam):
    B, S, C = x.shape
    xf = x.astype(jnp.float32)
    xb = xf.reshape(B, S, R_BLOCKS, R_BLOCK_DIM)
    r = jax.nn.sigmoid(jnp.einsum('bsnd,nde->bsne', xb, w_a.astype(jnp.float32)).reshape(B, S, C) + b_a.astype(jnp.float32))
    i = jax.nn.sigmoid(jnp.einsum('bsnd,nde->bsne', xb, w_x.astype(jnp.float32)).reshape(B, S, C) + b_x.astype(jnp.float32))
    log_a = -R_C * r * jax.nn.softplus(-lam.astype(jnp.float32))
    a = jnp.exp(log_a)
    u = jnp.sqrt(-jnp.expm1(2.0 * log_a)) * (i * xf)

    def combine(left, right):
        a1, b1 = left
        a2, b2 = right
        return a1 * a2, a2 * b1 + b2

    _, h = lax.associative_scan(combine, (a, u), axis=1)
    return h.astype(x.dtype)

def dsa_attention(q, k, v, q_idx, k_idx, w_idx):
    B, S, H, Dh = q.shape
    f32 = jnp.float32
    top_k = min(TOPK_MAX, S // 4)
    nb = S // Q_BLOCK
    key_pos = jnp.arange(S, dtype=jnp.int32)
    k_idx_f = k_idx.astype(f32)

    def blocks(t):
        return jnp.moveaxis(t.reshape((B, nb, Q_BLOCK) + t.shape[2:]), 1, 0)

    def attend(args):
        qb, qib, wb, start = args
        qpos = start + jnp.arange(Q_BLOCK, dtype=jnp.int32)
        visible = key_pos[None, None, :] <= qpos[None, :, None]
        logits = jnp.einsum('bqhd,bsd->bqhs', qib.astype(f32), k_idx_f) * (IDX_DIM ** -0.5)
        score = jnp.einsum('bqh,bqhs->bqs', wb.astype(f32) * (IDX_HEADS ** -0.5), jax.nn.relu(logits))
        score = jnp.where(visible, score, -jnp.inf)
        _, idx = lax.top_k(score, top_k)
        k_sel = jax.vmap(lambda kk, ii: kk[ii])(k, idx)
        v_sel = jax.vmap(lambda vv, ii: vv[ii])(v, idx)
        att = jnp.einsum('bqhd,bqkhd->bqhk', qb.astype(f32), k_sel.astype(f32)) * (Dh ** -0.5)
        keep = (idx <= qpos[None, :, None])[:, :, None, :]
        p = jax.nn.softmax(jnp.where(keep, att, -jnp.inf), axis=-1)
        return jnp.einsum('bqhk,bqkhd->bqhd', p, v_sel.astype(f32)).astype(q.dtype)

    starts = jnp.arange(nb, dtype=jnp.int32) * Q_BLOCK
    out = lax.map(attend, (blocks(q), blocks(q_idx), blocks(w_idx), starts))
    return jnp.moveaxis(out, 0, 1).reshape(B, S, H, Dh)

def first_inputs(seed: int = 0) -> dict:
    key = jax.random.key(seed)
    ks = jax.random.split(key, 24)
    f32 = jnp.float32

    def normal(k, shape, scale):
        return jax.random.normal(k, shape, f32) * scale

    def gain(k, shape):
        return 1.0 + 0.02 * jax.random.normal(k, shape, f32)

    x = normal(ks[0], (BATCH, SEQ, D_MODEL), 1.0)
    positions = (jnp.arange(SEQ, dtype=jnp.int32)[None, :]
                 + jax.random.randint(ks[1], (BATCH, 1), 0, 4096, dtype=jnp.int32))
    norm_mix = gain(ks[2], (DEPTH, D_MODEL))
    w_in = normal(ks[3], (DEPTH, D_MODEL, N_IN), D_MODEL ** -0.5)
    mlstm_conv_w = normal(ks[4], (DEPTH, M_CONV, 2 * D_BRANCH), M_CONV ** -0.5)
    mlstm_conv_b = normal(ks[5], (DEPTH, 2 * D_BRANCH), 0.02)
    mlstm_i_bias = normal(ks[6], (DEPTH, M_HEADS), 0.1)
    mlstm_f_bias = jnp.linspace(3.0, 6.0, M_HEADS, dtype=f32)[None, :] + normal(ks[7], (DEPTH, M_HEADS), 0.1)
    mlstm_norm = gain(ks[8], (DEPTH, D_BRANCH))
    rglru_conv_w = normal(ks[9], (DEPTH, R_CONV, D_BRANCH), R_CONV ** -0.5)
    rglru_conv_b = normal(ks[10], (DEPTH, D_BRANCH), 0.02)
    rglru_w_a = normal(ks[11], (DEPTH, R_BLOCKS, R_BLOCK_DIM, R_BLOCK_DIM), R_BLOCK_DIM ** -0.5)
    rglru_b_a = normal(ks[12], (DEPTH, D_BRANCH), 0.02)
    rglru_w_x = normal(ks[13], (DEPTH, R_BLOCKS, R_BLOCK_DIM, R_BLOCK_DIM), R_BLOCK_DIM ** -0.5)
    rglru_b_x = normal(ks[14], (DEPTH, D_BRANCH), 0.02)
    a_c = jax.random.uniform(ks[15], (DEPTH, D_BRANCH), f32, 0.9, 0.999)
    sig = a_c ** (1.0 / R_C)
    rglru_lambda = jnp.log(sig) - jnp.log1p(-sig)
    w_branch = normal(ks[16], (DEPTH, 3, D_BRANCH, D_MODEL), D_BRANCH ** -0.5)
    w_out = normal(ks[17], (DEPTH, D_MODEL, D_MODEL), D_MODEL ** -0.5)
    norm_ffn = gain(ks[18], (DEPTH, D_MODEL))
    ffn_up = normal(ks[19], (DEPTH, D_MODEL, 2 * D_FF), D_MODEL ** -0.5)
    ffn_conv_w = normal(ks[20], (DEPTH, FFN_CONV, D_FF), FFN_CONV ** -0.5)
    ffn_conv_b = normal(ks[21], (DEPTH, D_FF), 0.02)
    ffn_down = normal(ks[22], (DEPTH, D_FF, D_MODEL), D_FF ** -0.5)
    norm_final = gain(ks[23], (D_MODEL,))
    return {'x': x, 'positions': positions, 'norm_mix': norm_mix, 'w_in': w_in,
            'mlstm_conv_w': mlstm_conv_w, 'mlstm_conv_b': mlstm_conv_b,
            'mlstm_i_bias': mlstm_i_bias, 'mlstm_f_bias': mlstm_f_bias, 'mlstm_norm': mlstm_norm,
            'rglru_conv_w': rglru_conv_w, 'rglru_conv_b': rglru_conv_b,
            'rglru_w_a': rglru_w_a, 'rglru_b_a': rglru_b_a, 'rglru_w_x': rglru_w_x, 'rglru_b_x': rglru_b_x,
            'rglru_lambda': rglru_lambda, 'w_branch': w_branch, 'w_out': w_out, 'norm_ffn': norm_ffn,
            'ffn_up': ffn_up, 'ffn_conv_w': ffn_conv_w, 'ffn_conv_b': ffn_conv_b, 'ffn_down': ffn_down,
            'norm_final': norm_final}

def first_block(x, positions, norm_mix, w_in, mlstm_conv_w, mlstm_conv_b, mlstm_i_bias, mlstm_f_bias,
              mlstm_norm, rglru_conv_w, rglru_conv_b, rglru_w_a, rglru_b_a, rglru_w_x, rglru_b_x,
              rglru_lambda, w_branch, w_out, norm_ffn, ffn_up, ffn_conv_w, ffn_conv_b, ffn_down,
              norm_final):
    B, S, _ = x.shape
    cos, sin = rope_tables(positions, A_HEAD_DIM)
    split_at = np.cumsum(IN_SPLITS)[:-1].tolist()
    m_shape = (B, S, M_HEADS, M_HEAD_DIM)
    a_shape = (B, S, A_HEADS, A_HEAD_DIM)
    for l in range(DEPTH):
        h = rms_norm(x, norm_mix[l])
        (m_qk, m_v, m_o, m_i, m_f, r_x, r_g, a_q, a_k, a_v, a_qi, a_ki, a_w, gates) = jnp.split(
            h @ w_in[l], split_at, axis=-1)
        m_qk = jax.nn.silu(causal_dwconv(m_qk, mlstm_conv_w[l], mlstm_conv_b[l]))
        m_q, m_k = jnp.split(m_qk, 2, axis=-1)
        h_m = mlstm_chunkwise(m_q.reshape(m_shape), m_k.reshape(m_shape), m_v.reshape(m_shape),
                              m_i + mlstm_i_bias[l], m_f + mlstm_f_bias[l])
        y_a = (head_layer_norm(h_m, mlstm_norm[l]) * jax.nn.sigmoid(m_o.astype(jnp.float32))).astype(x.dtype)
        r_x = causal_dwconv(r_x, rglru_conv_w[l], rglru_conv_b[l])
        y_b = jax.nn.gelu(r_g) * rg_lru(r_x, rglru_w_a[l], rglru_b_a[l], rglru_w_x[l], rglru_b_x[l], rglru_lambda[l])
        q_c = apply_rope(a_q.reshape(a_shape), cos, sin)
        k_c = apply_rope(a_k.reshape(a_shape), cos, sin)
        qi = apply_rope(a_qi.reshape(B, S, IDX_HEADS, IDX_DIM), cos, sin)
        ki = apply_rope(a_ki[:, :, None, :], cos, sin)[:, :, 0, :]
        y_c = dsa_attention(q_c, k_c, a_v.reshape(a_shape), qi, ki, a_w).reshape(B, S, D_BRANCH)
        g_a, g_b, g_c = jnp.split(jax.nn.sigmoid(gates), 3, axis=-1)
        merged = (g_a * (y_a @ w_branch[l, 0]) + g_b * (y_b @ w_branch[l, 1])
                  + g_c * (y_c @ w_branch[l, 2]))
        x = x + merged @ w_out[l]
        h = rms_norm(x, norm_ffn[l])
        ff_g, ff_u = jnp.split(h @ ffn_up[l], 2, axis=-1)
        ff_g = causal_dwconv(ff_g, ffn_conv_w[l], ffn_conv_b[l])
        x = x + (jax.nn.gelu(ff_g) * ff_u) @ ffn_down[l]
    return rms_norm(x, norm_final)


CHUNK = 64

D_RWKV = D_MODEL // 2
HEAD_SIZE = 64
N_HEADS = D_RWKV // HEAD_SIZE
D_DECAY_LORA = max(32, int(round(1.8 * D_MODEL ** 0.5 / 32)) * 32)
D_AAA_LORA = max(32, int(round(1.8 * D_MODEL ** 0.5 / 32)) * 32)
D_MV_LORA = max(32, int(round(0.7 * D_MODEL ** 0.5 / 32)) * 32)
D_GATE_LORA = max(32, int(round(0.6 * D_MODEL ** 0.8 / 32)) * 32)

D_POOL = D_MODEL // 2
POOL_WINDOWS = (2, 4, 8, 16)
N_POOL_GROUPS = len(POOL_WINDOWS)
POOL_GROUP = D_POOL // N_POOL_GROUPS

D_FF_2 = ((8 * D_MODEL // 3 + 255) // 256) * 256

N_SHIFT = 3 * D_RWKV + D_DECAY_LORA + D_AAA_LORA + D_GATE_LORA
N_IN_2 = N_SHIFT + D_POOL + 2 * D_MODEL
N_MOD = 6 * D_MODEL

EPS_RMS = 1e-6
EPS_GN = 64e-5


def rms_norm_2(x, g):
    xf = x.astype(jnp.float32)
    y = xf * lax.rsqrt(jnp.mean(xf * xf, axis=-1, keepdims=True) + EPS_RMS)
    return (y * g.astype(jnp.float32)).astype(x.dtype)

def token_shift(z, mu):
    prev = jnp.pad(z, ((0, 0), (1, 0), (0, 0)))[:, :-1]
    return z + (prev - z) * mu

def wkv7_scan(r, w, k, v, kk, a):
    B, S, H, N = r.shape

    def to_chunks(t):
        return jnp.moveaxis(t, 1, 0).reshape(S // CHUNK, CHUNK, B, H, N)

    def step(state, inp):
        r_t, w_t, k_t, v_t, kk_t, a_t = inp
        sk = jnp.einsum('bhvk,bhk->bhv', state, kk_t)
        state = (state * w_t[:, :, None, :]
                 - sk[..., None] * (a_t * kk_t)[:, :, None, :]
                 + v_t[..., None] * k_t[:, :, None, :])
        return state, jnp.einsum('bhvk,bhk->bhv', state, r_t)

    def chunk_step(state, chunk_inp):
        return lax.scan(step, state, chunk_inp)

    state0 = jnp.zeros((B, H, N, N), jnp.float32)
    _, ys = lax.scan(chunk_step, state0, tuple(to_chunks(t) for t in (r, w, k, v, kk, a)))
    return jnp.moveaxis(ys.reshape(S, B, H, N), 0, 1)

def rwkv7_time_mix(ps, vl, v_first, w0, w_up, a0, a_up, v0, v_up, g_up, k_k, k_a, r_k, lnx_g, lnx_b):
    B, S, _ = ps.shape
    dt = ps.dtype
    f32 = jnp.float32
    o = 0
    r = ps[..., o:o + D_RWKV]; o += D_RWKV
    k = ps[..., o:o + D_RWKV]; o += D_RWKV
    v = ps[..., o:o + D_RWKV]; o += D_RWKV
    wl = ps[..., o:o + D_DECAY_LORA]; o += D_DECAY_LORA
    al = ps[..., o:o + D_AAA_LORA]; o += D_AAA_LORA
    gl = ps[..., o:o + D_GATE_LORA]

    log_w = -jax.nn.softplus(-(w0 + jnp.tanh(wl) @ w_up)) - 0.5
    decay = jnp.exp(-jnp.exp(log_w.astype(f32)))
    a = jax.nn.sigmoid(a0 + al @ a_up)
    g = jax.nn.sigmoid(gl) @ g_up
    if vl is None:
        v_first = v
    else:
        v = v + (v_first - v) * jax.nn.sigmoid(v0 + vl @ v_up)

    def heads(t):
        return t.reshape(B, S, N_HEADS, HEAD_SIZE).astype(f32)

    kk = heads(k * k_k)
    kk = kk / jnp.maximum(jnp.sqrt(jnp.sum(kk * kk, axis=-1, keepdims=True)), 1e-12)
    k = k * (1 + (a - 1) * k_a)
    r_h, k_h, v_h, a_h, w_h = heads(r), heads(k), heads(v), heads(a), heads(decay)

    y = wkv7_scan(r_h, w_h, k_h, v_h, kk, a_h)
    mean = jnp.mean(y, axis=-1, keepdims=True)
    var = jnp.mean(jnp.square(y - mean), axis=-1, keepdims=True)
    y = (y - mean) * lax.rsqrt(var + EPS_GN)
    y = y.reshape(B, S, D_RWKV) * lnx_g.astype(f32) + lnx_b.astype(f32)
    bonus = jnp.sum(r_h * k_h * r_k.astype(f32), axis=-1, keepdims=True) * v_h
    y = (y + bonus.reshape(B, S, D_RWKV)) * g.astype(f32)
    return y.astype(dt), v_first

def multiscale_pool(z, pool_w, pool_scale):
    B, S, _ = z.shape
    zg = z.reshape(B, S, N_POOL_GROUPS, POOL_GROUP).astype(jnp.float32)
    cs = jnp.cumsum(zg, axis=1)
    pos = jnp.arange(1, S + 1, dtype=jnp.float32)
    means = []
    for gi, win in enumerate(POOL_WINDOWS):
        cg = cs[:, :, gi]
        lower = jnp.pad(cg, ((0, 0), (win, 0), (0, 0)))[:, :S]
        count = jnp.minimum(pos, float(win))[None, :, None]
        means.append((cg - lower) / count)
    pooled = (jnp.stack(means, axis=2) - zg).astype(z.dtype)
    y = jnp.einsum('bsgc,gcd->bsgd', pooled, pool_w)
    return y.reshape(B, S, D_POOL) * pool_scale

def second_inputs(seed: int = 0) -> dict:
    key = jax.random.key(seed)
    ks = iter(jax.random.split(key, 32))
    f32 = jnp.float32

    def nrm(shape, s):
        return jax.random.normal(next(ks), shape, f32) * s

    def uni(shape, lo, hi):
        return jax.random.uniform(next(ks), shape, f32, lo, hi)

    L, Lv = DEPTH, DEPTH - 1
    return {
        "x": nrm((BATCH, SEQ, D_MODEL), 1.0),
        "c": nrm((BATCH, D_MODEL), 1.0),
        "ada_w": nrm((L, D_MODEL, N_MOD), 0.5 * D_MODEL ** -0.5),
        "ada_b": nrm((L, N_MOD), 0.1),
        "norm1_g": 1.0 + nrm((L, D_MODEL), 0.1),
        "w_in": nrm((L, D_MODEL, N_IN_2), D_MODEL ** -0.5),
        "v_down": nrm((Lv, D_MODEL, D_MV_LORA), D_MODEL ** -0.5),
        "mu_shift": uni((L, N_SHIFT), 0.0, 1.0),
        "mu_v": uni((Lv, D_MV_LORA), 0.0, 1.0),
        "w0": uni((L, D_RWKV), -6.0, -1.0),
        "w_up": nrm((L, D_DECAY_LORA, D_RWKV), 0.5 * D_DECAY_LORA ** -0.5),
        "a0": nrm((L, D_RWKV), 0.1),
        "a_up": nrm((L, D_AAA_LORA, D_RWKV), 0.5 * D_AAA_LORA ** -0.5),
        "v0": nrm((Lv, D_RWKV), 0.1),
        "v_up": nrm((Lv, D_MV_LORA, D_RWKV), 0.5 * D_MV_LORA ** -0.5),
        "g_up": nrm((L, D_GATE_LORA, D_RWKV), D_GATE_LORA ** -0.5),
        "k_k": 0.85 + nrm((L, D_RWKV), 0.05),
        "k_a": 1.0 + nrm((L, D_RWKV), 0.05),
        "r_k": nrm((L, N_HEADS, HEAD_SIZE), 0.1),
        "lnx_g": 1.0 + nrm((L, D_RWKV), 0.1),
        "lnx_b": nrm((L, D_RWKV), 0.02),
        "pool_w": nrm((L, N_POOL_GROUPS, POOL_GROUP, POOL_GROUP), POOL_GROUP ** -0.5),
        "pool_scale": 1.0 + nrm((L, D_POOL), 0.1),
        "proj_a": nrm((L, D_RWKV, D_MODEL), D_RWKV ** -0.5),
        "proj_b": nrm((L, D_POOL, D_MODEL), D_POOL ** -0.5),
        "w_out": nrm((L, D_MODEL, D_MODEL), D_MODEL ** -0.5),
        "norm2_g": 1.0 + nrm((L, D_MODEL), 0.1),
        "w_gu": nrm((L, D_MODEL, 2 * D_FF_2), D_MODEL ** -0.5),
        "w_down": nrm((L, D_FF_2, D_MODEL), D_FF_2 ** -0.5),
        "final_g": 1.0 + nrm((D_MODEL,), 0.1),
    }

def second_block(x, c, ada_w, ada_b, norm1_g, w_in, v_down, mu_shift, mu_v, w0, w_up, a0, a_up, v0, v_up,
              g_up, k_k, k_a, r_k, lnx_g, lnx_b, pool_w, pool_scale, proj_a, proj_b, w_out, norm2_g,
              w_gu, w_down, final_g):
    B, S, D = x.shape
    c_act = jax.nn.silu(c)
    v_first = None
    for l in range(DEPTH):
        mod = c_act @ ada_w[l] + ada_b[l]
        sh1, sc1, gt1, sh2, sc2, gt2 = [m[:, None, :] for m in jnp.split(mod, 6, axis=-1)]

        h = rms_norm_2(x, norm1_g[l]) * (1 + sc1) + sh1
        if l == 0:
            p = h @ w_in[0]
            vl = None
        else:
            p = h @ jnp.concatenate([w_in[l], v_down[l - 1]], axis=1)
            vl = token_shift(p[..., N_IN_2:], mu_v[l - 1])
        ps = token_shift(p[..., :N_SHIFT], mu_shift[l])
        z_pool = p[..., N_SHIFT:N_SHIFT + D_POOL]
        br_gate = jax.nn.sigmoid(p[..., N_SHIFT + D_POOL:N_IN_2]).reshape(B, S, 2, D)

        y_a, v_first = rwkv7_time_mix(ps, vl, v_first, w0[l], w_up[l], a0[l], a_up[l],
                                      None if l == 0 else v0[l - 1], None if l == 0 else v_up[l - 1],
                                      g_up[l], k_k[l], k_a[l], r_k[l], lnx_g[l], lnx_b[l])
        y_b = multiscale_pool(z_pool, pool_w[l], pool_scale[l])
        mixed = br_gate[:, :, 0] * (y_a @ proj_a[l]) + br_gate[:, :, 1] * (y_b @ proj_b[l])
        x = x + gt1 * (mixed @ w_out[l])

        h2 = rms_norm_2(x, norm2_g[l]) * (1 + sc2) + sh2
        gate, up = jnp.split(h2 @ w_gu[l], 2, axis=-1)
        x = x + gt2 * ((jax.nn.silu(gate) * up) @ w_down[l])
    return rms_norm_2(x, final_g)


def setup_inputs(seed=0):
    out = dict(first_inputs(seed))
    for name, value in second_inputs(seed + 1).items():
        if name != "x":
            out[name + "_2"] = value
    return out


def reference(
    x, positions, norm_mix, w_in, mlstm_conv_w, mlstm_conv_b, mlstm_i_bias, mlstm_f_bias,
    mlstm_norm, rglru_conv_w, rglru_conv_b, rglru_w_a, rglru_b_a, rglru_w_x, rglru_b_x,
    rglru_lambda, w_branch, w_out, norm_ffn, ffn_up, ffn_conv_w, ffn_conv_b, ffn_down,
    norm_final, c_2, ada_w_2, ada_b_2, norm1_g_2, w_in_2, v_down_2, mu_shift_2, mu_v_2, w0_2,
    w_up_2, a0_2, a_up_2, v0_2, v_up_2, g_up_2, k_k_2, k_a_2, r_k_2, lnx_g_2, lnx_b_2, pool_w_2,
    pool_scale_2, proj_a_2, proj_b_2, w_out_2, norm2_g_2, w_gu_2, w_down_2, final_g_2,
):
    x = first_block(
        x, positions, norm_mix, w_in, mlstm_conv_w, mlstm_conv_b, mlstm_i_bias, mlstm_f_bias,
        mlstm_norm, rglru_conv_w, rglru_conv_b, rglru_w_a, rglru_b_a, rglru_w_x, rglru_b_x,
        rglru_lambda, w_branch, w_out, norm_ffn, ffn_up, ffn_conv_w, ffn_conv_b, ffn_down,
        norm_final,
    )
    return second_block(
        x, c_2, ada_w_2, ada_b_2, norm1_g_2, w_in_2, v_down_2, mu_shift_2, mu_v_2, w0_2, w_up_2,
        a0_2, a_up_2, v0_2, v_up_2, g_up_2, k_k_2, k_a_2, r_k_2, lnx_g_2, lnx_b_2, pool_w_2,
        pool_scale_2, proj_a_2, proj_b_2, w_out_2, norm2_g_2, w_gu_2, w_down_2, final_g_2,
    )


_drawn_inputs = setup_inputs


def setup_inputs(seed=0):
    import zlib

    import numpy as np

    out = dict(_drawn_inputs(seed))
    spreads = {}
    factors = {'mlstm_conv_b': 5.5,
     'mlstm_i_bias': 64.0,
     'mlstm_norm': 5.305,
     'rglru_b_a': 44.713,
     'rglru_b_x': 23.775,
     'ffn_conv_b': 3.239,
     'norm_final': 2.729,
     'v_down_2': 2.987,
     'mu_v_2': 7.021,
     'w_up_2': 8.0,
     'a0_2': 8.0,
     'v0_2': 64.0,
     'v_up_2': 2.956,
     'k_k_2': 15.22,
     'k_a_2': 4.192,
     'lnx_g_2': 10.987,
     'lnx_b_2': 60.595,
     'pool_scale_2': 9.388,
     'norm_ffn': 4.118,
     'norm2_g_2': 3.491}
    for name, (base, spread) in spreads.items():
        noise = np.random.default_rng([zlib.crc32(name.encode()), seed]).standard_normal(out[name].shape)
        drawn = base * np.exp(spread * noise) if base else spread * noise
        out[name] = __import__('jax').numpy.asarray(drawn.astype(out[name].dtype))
    for name, factor in factors.items():
        out[name] = (out[name] * factor).astype(out[name].dtype)
    return out
```

```python
import math
from contextlib import ExitStack, contextmanager

import numpy as np
import concourse.bass as bass
from concourse import mybir

FP32 = mybir.dt.float32
FP32R = mybir.dt.float32r
ALU = mybir.AluOpType
ACT = mybir.ActivationFunctionType
AX = mybir.AxisListType

P = 128
D = 1024
S = 512
DEPTH = 2
KD = D // P
ST = S // P
DB = 512
BT = DB // P
SLOT = 256
M_HEADS = 4
A_HEADS = 8
TOP_K = min(256, S // 4)
EPS = 1e-6
EPS_GN = 64e-5
NEG = -1e30
TAKEN = -3e38
D_FF = 3 * D
FT = D_FF // P
D_FF2 = 2816
FT2 = D_FF2 // P
CH = 64
NCH = S // CH
NP = 4

C_MQK, C_MV, C_MO, C_MIF, C_RX, C_RG = 0, 1024, 1536, 2048, 2056, 2568
C_AQ, C_AV, C_AQI, C_AKI, C_AW, C_GATE = 3080, 4104, 4616, 5128, 5192, 5200
C2_R, C2_LORA, C2_GL1, C2_POOL, C2_GATE = 0, 1536, 1792, 1824, 2336

CONST_COLS = {}


def constants():
    p = np.arange(P)[:, None]
    c = np.arange(P)[None, :]
    q = p % CH
    f = np.arange(CH)[None, :]
    cols = {}
    cols["ident"] = (p == c)
    cols["ones"] = np.ones((P, P))
    cols["causal_st"] = (c >= p)
    cols["causal_neg"] = np.where(c <= p, 0.0, NEG)
    cols["blockones"] = (p // CH == c // CH)
    cols["ident2"] = (q == f)
    cols["lower"] = (f < q)
    cols["upper"] = (f > q)
    cols["upper_eq"] = (f >= q)
    for s in (1, 2, 4, 8, 16, 32):
        cols[f"level{s}"] = (q // (2 * s) == f // (2 * s)) & ((q // s) % 2 == 1) & ((f // s) % 2 == 0)
        if s == 1:
            cols["levelT1"] = (q // (2 * s) == f // (2 * s)) & ((f // s) % 2 == 1) & ((q // s) % 2 == 0)
    inv = (10000.0 ** (-np.arange(0, 64, 2, dtype=np.float32) / 64)).astype(np.float32)
    cols["freq"] = inv[np.arange(P) % 32][:, None]
    cols["rope_sign"] = np.where(p % 64 < 32, -1.0, 1.0)
    win = np.array([2, 4, 8, 16])[:, None]
    count = 1.0 / np.minimum(np.arange(1, 17)[None, :], win)
    cols["inv_count"] = np.broadcast_to(count.reshape(1, 64), (P, 64))
    at = 0
    parts = []
    for name, a in cols.items():
        a = np.asarray(a, np.float32)
        CONST_COLS[name] = (at, at + a.shape[1])
        at += a.shape[1]
        parts.append(a)
    return np.ascontiguousarray(np.concatenate(parts, axis=1))


class Core:

    def __init__(self, nc, ctx):
        self.nc, self.ctx = nc, ctx
        self.sems = {}
        self.used = []

    def sb(self, name, shape, dt=FP32):
        return self.ctx.enter_context(self.nc.sbuf_tensor(name, shape, dt))

    def sem(self, name):
        if name not in self.sems:
            self.sems[name] = self.ctx.enter_context(self.nc.semaphore(name))
        if name not in self.used and not name.startswith("ring_"):
            self.used.append(name)
        return self.sems[name]

    @contextmanager
    def stage(self):
        with self.nc.Block() as block:
            yield block
        for name in self.used:
            self.nc.gpsimd.sem_clear(self.sems[name])
        self.used = []
        self.nc.all_engine_barrier()

    def clear_ring(self):
        for name, s in self.sems.items():
            if name.startswith("ring_"):
                self.nc.gpsimd.sem_clear(s)
        self.nc.all_engine_barrier()


class Ring:

    def __init__(self, core):
        self.core = core
        self.raw = core.sb("w_raw", [P, 2, 2048])
        self.hi = core.sb("w_hi", [P, 2, 2048], FP32R)
        self.lo = core.sb("w_lo", [P, 2, 2048], FP32R)
        self.loaded = [core.sem(f"ring_loaded{s}") for s in (0, 1)]
        self.split = [core.sem(f"ring_split{s}") for s in (0, 1)]
        self.tile = [core.sem(f"ring_tile{s}") for s in (0, 1)]
        self.done = [core.sem(f"ring_done{s}") for s in (0, 1)]
        self.bank_free = [core.sem(f"ring_bank_free{b}") for b in range(8)]

    def load(self, sp, u, parts):
        for s in (0, 1):
            if not (isinstance(u, int) and u == 0):
                sp.wait_ge(self.split[s], u)
            for dst, src in parts[s]:
                sp.dma_start(dst, src).then_inc(self.loaded[s], 16)

    def halve(self, pool, u, n_dma, views):
        nc = self.core.nc
        for s in (0, 1):
            pool.wait_ge(self.loaded[s], n_dma[s])
            if views[s] is None:
                continue
            if not (isinstance(u, int) and u == 0):
                pool.wait_ge(self.done[s], u)
            raw, hi, lo = views[s](self.raw[:, s]), views[s](self.hi[:, s]), views[s](self.lo[:, s])
            one = self.one.to_broadcast([P, raw.free_size()]) if len(raw.shape) == 2 else \
                self.one.unsqueeze(2).to_broadcast([P, raw.shape[1], raw.shape[2]])
            nc.gpsimd.tensor_tensor(hi, raw, one, ALU.mult)
            pool.drain()
            nc.gpsimd.tensor_tensor(lo, raw, hi.bitcast(FP32), ALU.subtract).then_inc(self.split[s], 1)


class Section:

    def __init__(self, name, pairs, src, view=None, dmas=(1, 1)):
        self.name, self.pairs, self.src, self.dmas = name, pairs, src, dmas
        self.view = view or ((lambda b: b), (lambda b: b))


class Schedule:

    def __init__(self, ring, sections):
        self.ring, self.sections = ring, sections
        self.u0, self.dma0 = {}, {}
        u, n = 0, [0, 0]
        for sec in sections:
            self.u0[sec.name], self.dma0[sec.name] = u, list(n)
            u += sec.pairs
            n = [n[s] + sec.pairs * sec.dmas[s] * 16 for s in (0, 1)]

    def _pair(self, eng, sec, i, kind):
        u = self.u0[sec.name] + i
        if kind == "load":
            self.ring.load(eng, u, [sec.src(i, s) for s in (0, 1)])
        else:
            n = [self.dma0[sec.name][s] + (i + 1) * (16 * sec.dmas[s]) for s in (0, 1)]
            self.ring.halve(eng, u, n, sec.view)

    def run(self, eng, kind, names):
        at = [s.name for s in self.sections].index(names[0])
        secs = self.sections[at:at + len(names)]
        after = self.sections[at + len(names):at + len(names) + 1]
        for n, sec in enumerate(secs):
            if n:
                self._pair(eng, sec, 0, kind)
            if sec.pairs == 2:
                self._pair(eng, sec, 1, kind)
            elif sec.pairs > 2:
                with eng.Fori(1, sec.pairs) as i:
                    self._pair(eng, sec, i, kind)
        for sec in after:
            self._pair(eng, sec, 0, kind)


def each(eng, n):
    @contextmanager
    def loop():
        if n == 1:
            yield 0
        else:
            with eng.Fori(0, n) as i:
                yield i
    return loop()


def three_pass(nc, out, w, a, first, last):
    (wh, wl), (ah, al) = w, a
    nc.tensor.matmul(out, wh, ah, start=first, stop=False)
    nc.tensor.matmul(out, wh, al, start=False, stop=False)
    return nc.tensor.matmul(out, wl, ah, start=False, stop=last)


class Kernel:

    def __init__(self, nc, ctx, const_dram):
        self.nc = nc
        self.core = core = Core(nc, ctx)
        self.ring = Ring(core)
        self.x = core.sb("x", [P, KD, S])
        self.hi = core.sb("act_hi", [P, KD, S], FP32R)
        self.lo = core.sb("act_lo", [P, KD, S], FP32R)
        self.const = core.sb("consts", [P, const_dram.shape[1]])
        self.cols = core.sb("param_cols", [P, 2, P])
        self.small = core.sb("small", [P, 300])
        self.arena = core.sb("arena", [P, 52, S])
        self.ring.one = self.c("ones")[:, 0:1]
        self.rows = self.arena[:, 44, 0:2 * P].rearrange("p (b n) -> p b n", b=2)
        pads = self.arena[:, 21:24, :].rearrange("p a n -> p (a n)")
        self.pad = [pads[:, 0:S + 16], pads[:, 600:600 + S + 16]]
        self.ps = ctx.enter_context(nc.psum_tensor("banks", [P, 8, S], FP32))

    def c(self, name):
        a, b = CONST_COLS[name]
        return self.const[:, a:b]

    def col(self, name, j=0):
        buf, row, _ = self.param_at[name]
        return self.cols[:, buf, row + j:row + j + 1]

    def load_params(self, eng, sem, table):
        self.param_at, at, n = {}, [0, 0], 0
        for name, buf, views in table:
            self.param_at[name] = (buf, at[buf], sum(v.shape[0] for v in views))
            for v in views:
                r, w = v.shape[0], v.shape[1]
                if eng is not None:
                    eng.dma_start(self.rows[at[buf]:at[buf] + r, buf, 0:w], v).then_inc(sem, 16)
                    if name == "mu_l2":
                        eng.dma_start(self.rows[at[buf]:at[buf] + r, buf, 32:64], self.mu_v).then_inc(sem, 16)
                at[buf] += r
                n += 2 if name == "mu_l2" else 1
        return n

    def pe_feature(self, pe, u, act=None, wait_banks=True):
        ring, hi, lo = self.ring, self.hi, self.lo
        for s in (0, 1):
            pe.wait_ge(ring.split[s], u + 1)
            wh = ring.hi[:, s].rearrange("p (k n) -> p k n", k=8)
            wl = ring.lo[:, s].rearrange("p (k n) -> p k n", k=8)
            for t in (0, 1):
                b = 2 * s + t
                if not (isinstance(u, int) and u == 0):
                    pe.wait_ge(ring.bank_free[b], u)
                for k in range(KD):
                    cols = slice(t * P, t * P + P)
                    last = three_pass(self.nc, self.ps[:, b, :], (wh[:, k, cols], wl[:, k, cols]),
                                      (hi[:, k, :], lo[:, k, :]), k == 0, k == KD - 1)
                last.then_inc(ring.done[s] if t else ring.tile[s], 1)

    def pe_token(self, pe, u):
        ring, hi, lo = self.ring, self.hi, self.lo
        for s in (0, 1):
            pe.wait_ge(ring.split[s], u + 1)
            wh = ring.hi[:, s].rearrange("p (k n) -> p k n", k=8)
            wl = ring.lo[:, s].rearrange("p (k n) -> p k n", k=8)
            for tt in range(ST):
                if s == 0:
                    pe.wait_ge(ring.bank_free[tt], u)
                rows = slice(tt * P, tt * P + P)
                out = self.ps[:, tt, s * SLOT:(s + 1) * SLOT]
                for k in range(KD):
                    last = three_pass(self.nc, out, (hi[:, k, rows], lo[:, k, rows]),
                                      (wh[:, k, :], wl[:, k, :]), k == 0, k == KD - 1)
                if tt == 1:
                    last.then_inc(ring.tile[s], 1)
                if tt == ST - 1:
                    last.then_inc(ring.done[s], 1)

    def norm(self, gain, scale=None, shift=None, params=None, final=False, mod_of=None):
        nc, core, ps, x = self.nc, self.core, self.ps, self.x
        T = self.arena
        sq = [T[:, 48, :], T[:, 49, :]]
        rstd, tmp = T[:, 50, :], [T[:, 51, :], T[:, 45, :]]
        n_par = self.load_params(None, None, params) if params else 0
        param_in, param_t, rows_zero = core.sem("param_in"), core.sem("param_t"), core.sem("rows_zero")
        sq_ok, ssum = core.sem("square_ok"), core.sem("sum_of_squares")
        ms_ok, root_ok, norm_ok, hi_ok = (core.sem("mean_square"), core.sem("root"), core.sem("normed"),
                                          core.sem("norm_hi"))
        lo_ok = self.norm_lo = core.sem("norm_lo")

        def sp_part(sp):
            if params:
                sp.wait_ge(rows_zero, 1)
                self.load_params(sp, param_in, params)

        def pe_part(pe):
            if params:
                pe.wait_ge(param_in, 16 * n_par)
                for b in (0, 1):
                    last = nc.tensor.transpose(ps[:, 6, b * P:(b + 1) * P], self.rows[:, b, :],
                                               self.c("ident"))
                last.then_inc(param_t, 1)
            for k in range(KD):
                pe.wait_ge(sq_ok, k + 1)
                nc.tensor.matmul(ps[:, 7, :], self.c("ones"), sq[k % 2], start=(k == 0),
                                 stop=(k == KD - 1)).then_inc(ssum, 1)

        def act_part(act):
            for k in range(KD):
                if k >= 2:
                    act.wait_ge(ssum, k - 1)
                nc.scalar.activation(sq[k % 2], x[:, k, :], ACT.Square).then_inc(sq_ok, 1)
            act.wait_ge(ms_ok, 1)
            nc.scalar.activation(rstd, rstd, ACT.Sqrt).then_inc(root_ok, 1)
            if not final:
                for k in range(KD):
                    act.wait_ge(norm_ok, k + 1)
                    nc.scalar.activation(self.hi[:, k, :], tmp[k % 2], ACT.Copy).then_inc(hi_ok, 1)

        def dve_part(dve):
            if params:
                nc.vector.memset(self.rows[:, :, :], 0.0).then_inc(rows_zero, 1)
                dve.wait_ge(param_t, 1)
                nc.vector.tensor_copy(self.cols[:, :, :],
                                      ps[:, 6, 0:2 * P].rearrange("p (b n) -> p b n", b=2))
                dve.drain()
            if mod_of is not None:
                buf, row, n = self.param_at[mod_of[1]]
                nc.vector.tensor_tensor(self.mod, mod_of[0], self.cols[:, buf, row:row + n], ALU.add)
                dve.drain()
            if scale is not None:
                buf, row, _ = self.param_at[gain]
                gs = self.small[:, 288:296]
                nc.vector.scalar_tensor_tensor(gs, scale, 1.0, self.cols[:, buf, row:row + KD],
                                               ALU.add, ALU.mult)
                dve.drain()
            dve.wait_ge(ssum, KD)
            nc.vector.tensor_scalar(rstd, ps[:, 7, :], 1.0 / D, EPS, ALU.mult, ALU.add).then_inc(ms_ok, 1)
            dve.wait_ge(root_ok, 1)
            nc.vector.reciprocal(rstd, rstd)
            dve.drain()

            def lo_of(k):
                dve.wait_ge(hi_ok, k + 1)
                nc.vector.tensor_tensor(self.lo[:, k, :], tmp[k % 2], self.hi[:, k, :].bitcast(FP32),
                                        ALU.subtract).then_inc(lo_ok, 1)
            for k in range(KD):
                gk = self.col(gain, k) if scale is None else self.small[:, 288 + k:289 + k]
                if final:
                    nc.vector.scalar_tensor_tensor(x[:, k, :], x[:, k, :], gk, rstd, ALU.mult, ALU.mult)
                    continue
                if k >= 2:
                    dve.drain()
                i = nc.vector.scalar_tensor_tensor(tmp[k % 2], x[:, k, :], gk, rstd, ALU.mult, ALU.mult)
                if shift is not None:
                    dve.drain()
                    i = nc.vector.tensor_scalar(tmp[k % 2], tmp[k % 2], shift(k), None, ALU.add)
                i.then_inc(norm_ok, 1)
                if k:
                    lo_of(k - 1)
            if not final:
                lo_of(KD - 1)

        return sp_part, pe_part, act_part, dve_part

    def stage_norm(self, gain, params):
        sp_n, pe_n, act_n, dve_n = self.norm(gain, params=params, final=True)
        with self.core.stage() as block:
            block.sync(sp_n)
            block.tensor(pe_n)
            block.scalar(act_n)
            block.vector(dve_n)

    def pe_first(self, pe, u, wait_banks=False):
        ring = self.ring
        for k in range(KD):
            pe.wait_ge(self.norm_lo, k + 1)
            for b in range(4):
                s, t = divmod(b, 2)
                if k == 0 and t == 0:
                    pe.wait_ge(ring.split[s], u + 1)
                if k == 0 and not (isinstance(u, int) and u == 0):
                    pe.wait_ge(ring.bank_free[b], u)
                w = [v[:, s].rearrange("p (k n) -> p k n", k=8)[:, k, t * P:t * P + P] for v in (ring.hi, ring.lo)]
                last = three_pass(self.nc, self.ps[:, b, :], w, (self.hi[:, k, :], self.lo[:, k, :]),
                                  k == 0, k == KD - 1)
                if k == KD - 1:
                    last.then_inc(ring.done[s] if t else ring.tile[s], 1)

    def outer_tail(self, block, name, slots, source, gate=None):
        nc, core, ring, ps = self.nc, self.core, self.ring, self.ps
        u0 = self.schedule.u0[name]
        pairs = (slots + 1) // 2
        hi_ok, pair_ok, outs = core.sem("operand_hi"), core.sem("operand_ready"), core.sem("outer_done")

        def program(pe, dve, act, i, s, first, last):
            u = u0 + i
            if act is not None:
                act.wait_ge(ring.done[s], u)
                nc.scalar.activation(self.hi[:, 2 * s:2 * s + 2, :], source(i, s), ACT.Copy).then_inc(hi_ok, 1)
            if dve is not None:
                dve.wait_ge(hi_ok, 2 * i + s + 1)
                nc.vector.tensor_tensor(self.lo[:, 2 * s:2 * s + 2, :], source(i, s),
                                        self.hi[:, 2 * s:2 * s + 2, :].bitcast(FP32),
                                        ALU.subtract).then_inc(pair_ok, 1)
            if pe is not None:
                pe.wait_ge(ring.split[s], u + 1)
                pe.wait_ge(pair_ok, 2 * i + s + 1)
                wh = ring.hi[:, s].rearrange("p (k n) -> p k n", k=2)
                wl = ring.lo[:, s].rearrange("p (k n) -> p k n", k=2)
                for kk in (0, 1):
                    for m in range(KD):
                        cols = slice(m * P, m * P + P)
                        ins = three_pass(nc, ps[:, m, :], (wh[:, kk, cols], wl[:, kk, cols]),
                                         (self.hi[:, 2 * s + kk, :], self.lo[:, 2 * s + kk, :]),
                                         first and kk == 0, last and kk == 1)
                        if kk == 0 and m == 0:
                            ins.then_inc(ring.tile[s], 1)
                        elif kk == 1 and m == KD - 1:
                            ins.then_inc(ring.done[s], 1)
                        elif last and kk == 1:
                            ins.then_inc(outs, 1)

        def run(pe=None, dve=None, act=None):
            eng = pe or dve or act
            for s in (0, 1):
                program(pe, dve, act, 0, s, s == 0, False)
            if pairs > 2:
                with eng.Fori(1, pairs - 1) as i:
                    for s in (0, 1):
                        program(pe, dve, act, i, s, False, False)
            for s in range(2 - slots % 2):
                program(pe, dve, act, pairs - 1, s, False, s == 1 - slots % 2)

        @block.tensor
        def _(pe):
            run(pe=pe)
            if slots % 2:
                pe.drain().then_inc(ring.tile[1], 1)
                pe.drain().then_inc(ring.done[1], 1)

        @block.scalar
        def _(act):
            run(act=act)

        @block.vector
        def _(dve):
            run(dve=dve)
            last_u = u0 + pairs - 1
            for m in range(KD):
                if m == KD - 1:
                    dve.wait_ge(ring.done[1 - slots % 2], last_u + 1)
                else:
                    dve.wait_ge(outs, m + 1)
                if gate is None:
                    i = nc.vector.tensor_tensor(self.x[:, m, :], self.x[:, m, :], ps[:, m, :], ALU.add)
                else:
                    i = nc.vector.scalar_tensor_tensor(self.x[:, m, :], ps[:, m, :], gate(m), self.x[:, m, :],
                                                       ALU.mult, ALU.add)
            dve.drain()
            for m in range(4):
                dve.sem_inc(ring.bank_free[m], pairs)

    def tiles(self, a, n):
        return self.arena[:, a:a + n, :]

    def wait_tile(self, eng, u, b):
        s, t = divmod(b, 2)
        eng.wait_ge((self.ring.done if t else self.ring.tile)[s], u + 1)

    def stage_merge(self, names, srcs, gates_at, acc_at, prod_at):
        nc, core, ring, ps, A = self.nc, self.core, self.ring, self.ps, self.arena
        u = self.schedule.u0["branch"]
        sem = core.sem
        y_hi, y_lo, out = sem("branch_hi"), sem("branch_lo"), sem("branch_tile")
        done = sem("branch_used")
        merged, used = sem("merged"), sem("branch_bank_free")
        acc = A[:, acc_at:acc_at + KD, :]
        prod = [A[:, prod_at, :], A[:, prod_at + 1, :]]
        n_br = len(srcs)
        with core.stage() as block:
            @block.sync
            def _(sp):
                self.schedule.run(sp, "load", names)

            @block.gpsimd
            def _(pool):
                self.schedule.run(pool, "halve", names)

            @block.scalar
            def _(act):
                for b in range(n_br):
                    if b == 2:
                        act.wait_ge(ring.done[1], u + 1)
                    dst = self.hi[:, 4 * (b % 2):4 * (b % 2) + 4, :]
                    nc.scalar.activation(dst, self.tiles(srcs[b], 4), ACT.Copy).then_inc(y_hi, 1)

            @block.tensor
            def _(pe):
                for b in range(n_br):
                    pe.wait_ge(y_lo, b + 1)
                    for s in (0, 1):
                        pe.wait_ge(ring.split[s], u + b + 1)
                        wh = ring.hi[:, s].rearrange("p (k n) -> p k n", k=4)
                        wl = ring.lo[:, s].rearrange("p (k n) -> p k n", k=4)
                        for t in range(4):
                            m = 4 * s + t
                            if b:
                                pe.wait_ge(used, 8 * (b - 1) + m + 1)
                            cols = slice(t * P, t * P + P)
                            for k in range(4):
                                kk = 4 * (b % 2) + k
                                last = three_pass(nc, ps[:, m, :], (wh[:, k, cols], wl[:, k, cols]),
                                                  (self.hi[:, kk, :], self.lo[:, kk, :]), k == 0, k == 3)
                            last.then_inc(ring.done[s] if t == 3 else out, 1)
                        pe.sem_inc(ring.tile[s], 1)

            @block.vector
            def _(dve):
                def lo_of(b):
                    dve.wait_ge(y_hi, b + 1)
                    hl = slice(4 * (b % 2), 4 * (b % 2) + 4)
                    nc.vector.tensor_tensor(self.lo[:, hl, :], self.tiles(srcs[b], 4),
                                            self.hi[:, hl, :].bitcast(FP32), ALU.subtract).then_inc(y_lo, 1)
                lo_of(0)
                lo_of(1)
                for b in range(n_br):
                    for m in range(KD):
                        s, t = divmod(m, 4)
                        if t == 3:
                            dve.wait_ge(ring.done[s], u + b + 1)
                        else:
                            dve.wait_ge(out, 6 * b + 3 * s + t + 1)
                        g = A[:, gates_at + 8 * b + m, :]
                        if b == 0:
                            nc.vector.tensor_tensor(acc[:, m, :], ps[:, m, :], g, ALU.mult).then_inc(used, 1)
                        else:
                            nc.vector.tensor_tensor(prod[m % 2], ps[:, m, :], g, ALU.mult).then_inc(used, 1)
                            dve.drain()
                            nc.vector.tensor_tensor(acc[:, m, :], acc[:, m, :], prod[m % 2], ALU.add)
                    if b == 0 and n_br == 3:
                        lo_of(2)
                dve.drain()
                for m in range(4):
                    dve.sem_inc(ring.bank_free[m], n_br)


    def stage_w_out(self, acc_at, gate=None):
        acc = self.arena[:, acc_at:acc_at + KD, :]
        with self.core.stage() as block:
            @block.sync
            def _(sp):
                self.schedule.run(sp, "load", ["w_out"])

            @block.gpsimd
            def _(pool):
                self.schedule.run(pool, "halve", ["w_out"])
            self.outer_tail(block, "w_out", 4, lambda i, s: acc[:, 4 * i + 2 * s:4 * i + 2 * s + 2, :], gate)

    def stage_ffn_down(self, names, slots, hid, gate=None):
        A = self.arena

        def hidden(i, s):
            if isinstance(i, int):
                return A[:, hid + 4 * i + 2 * s:hid + 4 * i + 2 * s + 2, :]
            return A[:, bass.ds(i * 4 + (hid + 2 * s), 2), :]
        with self.core.stage() as block:
            @block.sync
            def _(sp):
                self.schedule.run(sp, "load", names)

            @block.gpsimd
            def _(pool):
                self.schedule.run(pool, "halve", names)
            self.outer_tail(block, names[0], slots, hidden, gate)


def swapped(q):
    return q ^ 1


class First(Kernel):

    AQ, AK, AV, QI, KI, SC, YB, T = 0, 4, 8, 12, 16, 17, 21, 25
    conv_tiles = {'mconv': 8, 'rconv': 4}
    YA, YC = QI, AQ
    MQ, MK, MO, RX, RG, MV, GATES, HID = 28, 32, 36, 40, 44, 48, 28, 28

    def make_schedule(self, w_in, w_branch, w_out, ffn_up, ffn_down):
        ring = self.ring
        win = w_in.rearrange("(k p) n -> p k n", p=P)
        up = ffn_up.rearrange("(k p) n -> p k n", p=P)
        raw = [ring.raw[:, s].rearrange("p (k n) -> p k n", k=8) for s in (0, 1)]
        raw4 = [ring.raw[:, s].rearrange("p (k n) -> p k n", k=4) for s in (0, 1)]
        raw2 = [ring.raw[:, s].rearrange("p (k n) -> p k n", k=2) for s in (0, 1)]

        def columns(first):
            return lambda i, s: [(raw[s], win[:, :, bass.ds(i * 512 + first + s * SLOT, SLOT)])]

        def misc(i, s):
            if s == 0:
                return [(raw[0][:, :, 0:64], win[:, :, C_AKI:C_AKI + 64]),
                        (raw[0][:, :, 64:128], win[:, :, C_AKI:C_AKI + 64])]
            return [(raw[1][:, :, 0:8], win[:, :, C_MIF:C_MIF + 8]),
                    (raw[1][:, :, 8:16], win[:, :, C_AW:C_AW + 8])]

        def part(n):
            return lambda b: b.rearrange("p (k n) -> p k n", k=8)[:, :, 0:n]

        def up_cols(i, s):
            return [(raw[s], up[:, :, bass.ds(i * SLOT + s * D_FF, SLOT)])]

        def branch(i, s):
            wb = w_branch[i].rearrange("(k p) n -> p k n", p=P)
            return [(raw4[s], wb[:, :, s * 512:(s + 1) * 512])]

        def rows_of(w):
            v = w.rearrange("(q k p) n -> q p k n", p=P, k=2)
            return lambda i, s: [(raw2[s], v[2 * i + s])]

        self.schedule = Schedule(ring, [
            Section("misc", 1, misc, view=(part(128), part(16)), dmas=(2, 2)),
            Section("aqk", 2, columns(C_AQ)), Section("aqi", 1, columns(C_AQI)),
            Section("av", 1, columns(C_AV)),
            Section("mqk", 2, columns(C_MQK)), Section("mv", 1, columns(C_MV)),
            Section("mo", 1, columns(C_MO)), Section("rx", 1, columns(C_RX)),
            Section("rg", 1, columns(C_RG)),
            Section("gates", 6, columns(C_GATE)),
            Section("branch", 3, branch),
            Section("w_out", 2, rows_of(w_out)),
            Section("up", 12, up_cols),
            Section("down", 6, rows_of(ffn_down)),
        ])

    def stage_attention_inputs(self, rope_dram, params):
        sp_n, pe_n, act_n, dve_n = self.norm("norm_mix", params=params)
        nc, core, ring, ps = self.nc, self.core, self.ring, self.ps
        u = self.schedule.u0
        cos, sin = self.tiles(46, 2)[:, 0, :], self.tiles(46, 2)[:, 1, :]
        turned = [self.arena[:, self.T, :], self.arena[:, self.T + 1, :]]
        gate_tm = self.small[:, 0:64].rearrange("p (t c) -> p t c", t=ST)
        table_in, turn_ok, turn_used = core.sem("table_in"), core.sem("turned"), core.sem("turned_used")
        names = ["misc", "aqk", "aqi", "av"]

        def rope_act(act, n, u_, b, first=False):
            self.wait_tile(act, u_, b)
            act.wait_ge(turn_used, n)
            for q in range(4):
                i = nc.scalar.activation(turned[b % 2][32 * q:32 * q + 32, :],
                                         ps[32 * swapped(q):32 * swapped(q) + 32, b, :], ACT.Copy)
            i.then_inc(turn_ok, 1)

        def rope_dve(dve, n, dst, u_, b):
            dve.wait_ge(turn_ok, n)
            nc.vector.tensor_tensor(dst, ps[:, b, :], cos, ALU.mult).then_inc(ring.bank_free[b], 1)
            nc.vector.tensor_tensor(turned[b % 2], turned[b % 2], sin, ALU.mult)
            dve.drain()
            nc.vector.tensor_tensor(dst, dst, turned[b % 2], ALU.add).then_inc(turn_used, 1)

        with core.stage() as block:
            @block.sync
            def _(sp):
                sp_n(sp)
                self.schedule._pair(sp, self.schedule.sections[0], 0, "load")
                sp.dma_start(self.tiles(46, 2), rope_dram).then_inc(table_in, 16)
                self.schedule.run(sp, "load", names)

            @block.gpsimd
            def _(pool):
                self.schedule._pair(pool, self.schedule.sections[0], 0, "halve")
                self.schedule.run(pool, "halve", names)

            @block.tensor
            def _(pe):
                pe_n(pe)
                pe.wait_ge(ring.split[0], 1)
                for k in range(KD):
                    pe.wait_ge(self.norm_lo, k + 1)
                    wh, wl = (b[:, 0].rearrange("p (k n) -> p k n", k=8)[:, k, 0:128]
                              for b in (ring.hi, ring.lo))
                    last = three_pass(nc, ps[:, 1, :], (wh, wl), (self.hi[:, k, :], self.lo[:, k, :]),
                                      k == 0, k == KD - 1)
                last.then_inc(ring.done[0], 1)
                pe.wait_ge(ring.split[1], 1)
                for tt in range(ST):
                    rows = slice(tt * P, tt * P + P)
                    for k in range(KD):
                        wh, wl = (b[:, 1].rearrange("p (k n) -> p k n", k=8)[:, k, 0:16]
                                  for b in (ring.hi, ring.lo))
                        last = three_pass(nc, ps[:, 3, tt * 16:tt * 16 + 16],
                                          (self.hi[:, k, rows], self.lo[:, k, rows]), (wh, wl),
                                          k == 0, k == KD - 1)
                    if tt == 0:
                        last.then_inc(ring.tile[1], 1)
                    if tt == 1:
                        last.then_inc(ring.tile[0], 1)
                last.then_inc(ring.done[1], 1)
                with pe.Fori(0, 2) as i:
                    self.pe_feature(pe, i + u["aqk"])
                self.pe_feature(pe, u["aqi"])
                self.pe_token(pe, u["av"])

            @block.scalar
            def _(act):
                act_n(act)
                self.wait_tile(act, 0, 1)
                for q in range(4):
                    i = nc.scalar.activation(turned[1][32 * q:32 * q + 32, :],
                                             ps[32 * swapped(q):32 * swapped(q) + 32, 1, :], ACT.Copy)
                i.then_inc(turn_ok, 1)
                with act.Fori(0, 2) as j:
                    for b in range(4):
                        rope_act(act, j * 4 + (b + 2), j + u["aqk"], b)
                for b in range(4):
                    rope_act(act, 8 + b + 2, u["aqi"], b)
                for b in range(4):
                    self.wait_tile(act, u["av"], 3)
                    nc.scalar.activation(self.arena[:, self.AV + b, :], ps[:, b, :], ACT.Copy)\
                        .then_inc(ring.bank_free[b], 1)

            @block.vector
            def _(dve):
                dve_n(dve)
                dve.sem_inc(turn_used, 2)
                dve.wait_ge(table_in, 16)
                rope_dve(dve, 1, self.arena[:, self.KI, :], 0, 1)
                dve.wait_ge(ring.done[1], 1)
                nc.vector.tensor_copy(gate_tm, ps[:, 3, 0:64].rearrange("p (t c) -> p t c", t=ST))\
                    .then_inc(ring.bank_free[3], 1)
                dve.drain()
                nc.vector.tensor_scalar(gate_tm[:, :, 8:16], gate_tm[:, :, 8:16], A_HEADS ** -0.5, None, ALU.mult)
                dve.sem_inc(ring.bank_free[0], 1)
                dve.sem_inc(ring.bank_free[2], 1)
                with dve.Fori(0, 2) as j:
                    for b in range(4):
                        dst = self.arena[:, bass.ds(j * 4 + (self.AQ + b), 1), :].rearrange("p a n -> p (a n)")
                        rope_dve(dve, j * 4 + (b + 2), dst, j + u["aqk"], b)
                for b in range(4):
                    rope_dve(dve, 8 + b + 2, self.arena[:, self.QI + b, :], u["aqi"], b)

    def stage_branch_inputs(self):
        nc, core, ring, ps = self.nc, self.core, self.ring, self.ps
        u = self.schedule.u0
        names = ["mqk", "mv", "mo", "rx", "rg"]
        pad = self.pad
        gate_tm = self.small[:, 0:64].rearrange("p (t c) -> p t c", t=ST)
        best = self.small[:, 64:72]
        relu = [self.arena[:, self.T + 1, :], self.arena[:, self.T + 2, :]]
        work = self.arena[:, self.T, :]
        logits, relu_ok, relu_used = core.sem("logits"), core.sem("relu_ok"), core.sem("relu_used")
        pad_ok, conv_ok, pad_zero = core.sem("pad_ok"), core.sem("conv_ok"), core.sem("pad_zero")

        def index_pe(pe, qt):
            n = (qt + 1) * P
            for h in range(A_HEADS):
                c = (ST - 1 - qt) * A_HEADS + h
                if c >= 2:
                    pe.wait_ge(relu_ok, c - 1)
                rows = slice(64 * (h % 2), 64 * (h % 2) + 64)
                nc.tensor.matmul(ps[:, 4 + c % 2, 0:n],
                                 self.arena[rows, self.QI + h // 2, qt * P:qt * P + P],
                                 self.arena[rows, self.KI, 0:n], start=True, stop=True).then_inc(logits, 1)

        def index_act(act, qt):
            n = (qt + 1) * P
            for h in range(A_HEADS):
                c = (ST - 1 - qt) * A_HEADS + h
                act.wait_ge(logits, c + 1)
                if c >= 2:
                    act.wait_ge(relu_used, c - 1)
                nc.scalar.activation(relu[c % 2][:, 0:n], ps[:, 4 + c % 2, 0:n], ACT.Relu,
                                     scale=64 ** -0.5).then_inc(relu_ok, 1)

        def index_dve(dve, qt):
            n = (qt + 1) * P
            score = self.arena[:, self.SC + qt, 0:n]
            for h in range(A_HEADS):
                c = (ST - 1 - qt) * A_HEADS + h
                w = gate_tm[:, qt, 8 + h:9 + h]
                dve.wait_ge(relu_ok, c + 1)
                if h == 0:
                    nc.vector.tensor_scalar(score, relu[c % 2][:, 0:n], w, None, ALU.mult).then_inc(relu_used, 1)
                else:
                    nc.vector.scalar_tensor_tensor(score, relu[c % 2][:, 0:n], w, score, ALU.mult, ALU.add)\
                        .then_inc(relu_used, 1)
                dve.drain()
            diag = score[:, qt * P:qt * P + P]
            nc.vector.tensor_tensor(diag, diag, self.c("causal_neg"), ALU.add)
            dve.drain()
            for r in range(TOP_K // 8):
                src = score if r == 0 else work[:, 0:n]
                nc.vector.max(best, src)
                dve.drain()
                nc.vector.match_replace(work[:, 0:n], best, src, TAKEN)
                dve.drain()
            nc.vector.tensor_scalar(score, work[:, 0:n], TAKEN / 2, NEG, ALU.is_ge, ALU.mult)

        def conv_dve(dve, n, b, w, j, dst, taps, jw):
            dve.wait_ge(pad_ok, n)
            src = pad[b % 2]
            nc.vector.tensor_scalar(dst, src[:, 0:S], self.col(w + "_w", jw), self.col(w + "_b", j),
                                    ALU.mult, ALU.add)
            for t in range(1, taps):
                dve.drain()
                i = nc.vector.scalar_tensor_tensor(dst, src[:, t:t + S], self.col(w + "_w", jw + t * self.conv_tiles[w]),
                                                   dst, ALU.mult, ALU.add)
            i.then_inc(conv_ok, 1)

        def silu_act(act, n):
            act.wait_ge(conv_ok, n)
            t = self.arena[:, self.MQ + n - 1, :]
            nc.scalar.activation(t, t, ACT.Silu)

        def pad_act(act, n, u_, b):
            self.wait_tile(act, u_, b)
            if n > 2:
                act.wait_ge(conv_ok, n - 2)
            nc.scalar.activation(pad[b % 2][:, 3:3 + S], ps[:, b, :], ACT.Copy).then_inc(ring.bank_free[b], 1)
            act.drain().then_inc(pad_ok, 1)

        with core.stage() as block:
            @block.sync
            def _(sp):
                self.schedule.run(sp, "load", names)

            @block.gpsimd
            def _(pool):
                self.schedule.run(pool, "halve", names)

            @block.tensor
            def _(pe):
                index_pe(pe, 3)
                self.pe_feature(pe, u["mqk"])
                self.pe_feature(pe, u["mqk"] + 1)
                index_pe(pe, 2)
                self.pe_token(pe, u["mv"])
                self.pe_token(pe, u["mo"])
                index_pe(pe, 1)
                self.pe_feature(pe, u["rx"])
                self.pe_feature(pe, u["rg"])

            @block.scalar
            def _(act):
                n = 0
                act.wait_ge(pad_zero, 1)
                index_act(act, 3)
                for j in range(8):
                    n += 1
                    pad_act(act, n, u["mqk"] + j // 4, j % 4)
                    if n >= 2:
                        silu_act(act, n - 1)
                silu_act(act, 8)
                index_act(act, 2)
                for b in range(4):
                    self.wait_tile(act, u["mv"], 3)
                    nc.scalar.activation(self.arena[:, self.MV + b, :], ps[:, b, :], ACT.Copy)\
                        .then_inc(ring.bank_free[b], 1)
                for b in range(4):
                    self.wait_tile(act, u["mo"], 3)
                    nc.scalar.activation(self.arena[:, self.MO + b, :], ps[:, b, :], ACT.Sigmoid)\
                        .then_inc(ring.bank_free[b], 1)
                index_act(act, 1)
                for j in range(4):
                    n += 1
                    pad_act(act, n, u["rx"], j)
                for b in range(4):
                    self.wait_tile(act, u["rg"], b)
                    nc.scalar.activation(self.arena[:, self.RG + b, :], ps[:, b, :], ACT.Gelu_apprx_tanh)\
                        .then_inc(ring.bank_free[b], 1)
            @block.vector
            def _(dve):
                for b in (0, 1):
                    nc.vector.memset(pad[b][:, 0:3], 0.0)
                dve.drain().then_inc(pad_zero, 1)
                index_dve(dve, 3)
                for j in range(8):
                    conv_dve(dve, j + 1, j, "mconv", j, self.arena[:, self.MQ + j, :], 4, j)
                index_dve(dve, 2)
                index_dve(dve, 1)
                for j in range(4):
                    conv_dve(dve, 9 + j, j, "rconv", j, self.arena[:, self.RX + j, :], 4, j)
                nc.vector.tensor_copy(self.arena[:, self.SC, 0:P], self.c("causal_neg"))

    def stage_mlstm_lru(self, i_bias, f_bias, w_a, w_x):
        nc, core, ps, A = self.nc, self.core, self.ps, self.arena
        gate_tm = self.small[:, 0:64].rearrange("p (t c) -> p t c", t=ST)
        am = self.small[:, 64:96].rearrange("p (t c) -> p t c", t=ST)
        bias = self.small[0:4, 96:98]
        den = self.small[:, 100:116]
        rcp = self.small[:, 116:132]
        stat = self.small[:, 132:148]
        enm = self.small[:, 148:164].rearrange("p (h t) -> p h t", h=4)
        lru_c = self.small[:, 164:168]
        poly = [self.small[:, 168 + 4 * j:172 + 4 * j] for j in range(4)]
        R0, R1, R2, R3 = (A[0:4, self.QI + j, :] for j in range(4))
        M_rows = R0
        off = [0, 512, 896, 1152]
        prob = A[:, self.T:self.T + 3, :].rearrange("p a n -> p (a n)")
        num = A[:, self.MQ:self.MQ + 4, :].rearrange("p h (t d) -> p (h t) d", t=ST)
        sqr = A[:, self.MK:self.MK + 4, :].rearrange("p h (t d) -> p (h t) d", t=ST)
        wax = A[:, self.KI, :].rearrange("p (m j e) -> p m j e", m=2, j=BT)
        sem = core.sem
        small_in, rows_t, neg_abs, soft = sem("small_in"), sem("gate_rows"), sem("forget_abs"), sem("softplus")
        am_rows, am_t, am_ok, enm_ok = sem("am_rows"), sem("am_transposed"), sem("am_ok"), sem("exp_neg_m")
        mb, score, gap, decay, p_ok, pv, pv_used = (sem("m_broadcast"), sem("score"), sem("gap"), sem("decay"),
                                                    sem("prob"), sem("pv"), sem("pv_used"))
        cent, sq_ok, var_ok, std_ok, y_ok, yt, yt_used = (sem("centred"), sem("squared"), sem("var"),
                                                          sem("std"), sem("y_tm"), sem("y_t"), sem("y_t_used"))
        elam, gates_ps, rl_ok, lru_th, lru_w, lru_a, lru_sq, lru_out = (
            sem("exp_lambda"), sem("lru_products"), sem("lru_gates"), sem("lru_tanh"), sem("lru_w"),
            sem("lru_a"), sem("lru_root"), sem("lru_out"))
        lam_neg = sem("lambda_abs")
        lru_coef = sem("lru_coef")
        SCALE = float(P) ** -0.5

        with core.stage() as block:
            @block.sync
            def _(sp):
                sp.dma_start(bias[:, 0:1], i_bias).then_inc(small_in, 16)
                sp.dma_start(bias[:, 1:2], f_bias).then_inc(small_in, 16)
                for m, w in ((0, w_a), (1, w_x)):
                    v = w.rearrange("(j q) d e -> q d j e", q=2)
                    for q in (0, 1):
                        sp.dma_start(wax[64 * q:64 * q + 64, m], v[q]).then_inc(small_in, 16)

            @block.tensor
            def _(pe):
                for tt in range(ST):
                    cols = slice(tt * P, tt * P + P)
                    nc.tensor.transpose(ps[0:4, 0, cols], gate_tm[:, tt, 0:4], self.c("ident"))
                    last = nc.tensor.transpose(ps[0:4, 1, cols], gate_tm[:, tt, 4:8], self.c("ident"))
                last.then_inc(rows_t, 1)
                pe.wait_ge(am_rows, 1)
                for tt in range(ST):
                    cols = slice(tt * P, tt * P + P)
                    nc.tensor.transpose(ps[:, 2, tt * 8:tt * 8 + 4], R1[:, cols], self.c("ident")[0:4, 0:4])
                    last = nc.tensor.transpose(ps[:, 2, tt * 8 + 4:tt * 8 + 8], R2[:, cols],
                                               self.c("ident")[0:4, 0:4])
                last.then_inc(am_t, 1)
                for h in range(M_HEADS):
                    if h:
                        pe.wait_ge(gap, 4 * h)
                    nc.tensor.matmul(ps[:, 3, :], self.c("ident")[0:4, h:h + 1].to_broadcast([4, P]), M_rows,
                                     start=True, stop=True).then_inc(mb, 1)
                    for j in range(ST):
                        n, k = S - j * P, 4 * h + j
                        if k >= 2:
                            pe.wait_ge(p_ok, k - 1)
                        nc.tensor.matmul(ps[:, 4 + k % 2, 0:n], A[:, self.MK + h, j * P:j * P + P],
                                         A[:, self.MQ + h, j * P:S], start=True, stop=True).then_inc(score, 1)
                    pe.wait_ge(p_ok, 4 * h + 4)
                    if h:
                        pe.wait_ge(pv_used, h)
                    for tt in range(ST):
                        for j in range(tt + 1):
                            lhs = prob[:, off[j] + (tt - j) * P:off[j] + (tt - j) * P + P]
                            nc.tensor.matmul(ps[:, 6, tt * P:tt * P + P], lhs,
                                             A[:, self.MV + j, h * P:h * P + P], start=(j == 0), stop=(j == tt))
                        for j in range(tt + 1):
                            lhs = prob[:, off[j] + (tt - j) * P:off[j] + (tt - j) * P + P]
                            last = nc.tensor.matmul(ps[:, 7, tt:tt + 1], lhs, self.c("ones")[:, 0:1],
                                                    start=(j == 0), stop=(j == tt))
                    last.then_inc(pv, 1)
                pe.wait_ge(small_in, 96)
                for j in range(BT):
                    if j:
                        pe.wait_ge(rl_ok, 2 * j)
                    for m in (0, 1):
                        for q in (0, 1):
                            r = slice(64 * q, 64 * q + 64)
                            last = nc.tensor.matmul(ps[r, m, :], wax[r, m, j, :], A[r, self.RX + j, :],
                                                    start=True, stop=True)
                    last.then_inc(gates_ps, 1)
                pe.wait_ge(y_ok, 1)
                for h in range(M_HEADS):
                    if h >= 2:
                        pe.wait_ge(yt_used, h - 1)
                    for tt in range(ST):
                        last = nc.tensor.transpose(ps[:, 4 + h % 2, tt * P:tt * P + P], num[:, h * ST + tt, :],
                                                   self.c("ident"))
                    last.then_inc(yt, 1)

            @block.scalar
            def _(act):
                act.wait_ge(neg_abs, 1)
                nc.scalar.activation(R2, R2, ACT.Exp, scale=-1.0)
                act.drain()
                nc.scalar.activation(R2, R2, ACT.Ln, bias=1.0).then_inc(soft, 1)
                act.wait_ge(am_ok, 1)
                nc.scalar.activation(enm, am[:, :, 4:8].rearrange("p t h -> p h t"), ACT.Exp, scale=-1.0)\
                    .then_inc(enm_ok, 1)
                act.wait_ge(lam_neg, 1)
                nc.scalar.activation(lru_c, lru_c, ACT.Exp, scale=-1.0).then_inc(elam, 1)
                for h in range(M_HEADS):
                    for j in range(ST):
                        n, k = S - j * P, 4 * h + j
                        act.wait_ge(gap, k + 1)
                        e = prob[:, off[j]:off[j] + n]
                        nc.scalar.activation(e, e, ACT.Exp, scale=-1.0).then_inc(decay, 1)
                act.wait_ge(cent, 1)
                nc.scalar.activation(sqr, num, ACT.Square).then_inc(sq_ok, 1)
                act.wait_ge(var_ok, 1)
                nc.scalar.activation(stat, stat, ACT.Sqrt).then_inc(std_ok, 1)
                act.wait_ge(lru_coef, 1)
                for j in range(BT):
                    act.wait_ge(gates_ps, j + 1)
                    if j:
                        act.wait_ge(lru_out, j)
                    nc.scalar.activation(A[:, self.T, :], ps[:, 0, :], ACT.Sigmoid, bias=self.col("lru_ba", j))\
                        .then_inc(rl_ok, 1)
                    nc.scalar.activation(A[:, self.T + 1, :], ps[:, 1, :], ACT.Sigmoid,
                                         bias=self.col("lru_bx", j)).then_inc(rl_ok, 1)
                    act.wait_ge(rl_ok, 2 * j + 2)
                    nc.scalar.activation(A[:, self.T + 2, :], A[:, self.T, :], ACT.Tanh,
                                         scale=lru_c[:, j:j + 1]).then_inc(lru_th, 1)
                    act.drain()
                    nc.scalar.activation(A[:, self.T, :], A[:, self.T, :], ACT.Exp, scale=poly[0][:, j:j + 1])\
                        .then_inc(lru_a, 1)
                    act.wait_ge(lru_w, j + 1)
                    nc.scalar.activation(A[:, self.T + 2, :], A[:, self.T + 2, :], ACT.Sqrt).then_inc(lru_sq, 1)
                for h in range(M_HEADS):
                    act.wait_ge(yt, h + 1)
                    nc.scalar.activation(A[:, self.YA + h, :], ps[:, 4 + h % 2, :], ACT.Copy,
                                         scale=self.col("mlstm_norm", h)).then_inc(yt_used, 1)

            @block.vector
            def _(dve):
                tt_, ts_, stt_ = nc.vector.tensor_tensor, nc.vector.tensor_scalar, nc.vector.scalar_tensor_tensor
                dve.wait_ge(small_in, 96)
                dve.wait_ge(rows_t, 1)
                ts_(R0, ps[0:4, 1, :], bias[:, 1:2], None, ALU.add)
                ts_(R1, ps[0:4, 0, :], bias[:, 0:1], None, ALU.add)
                nc.vector.memset(R3, 0.0)
                dve.drain()
                stt_(R2, R0, -1.0, R0, ALU.mult, ALU.max).then_inc(neg_abs, 1)
                dve.wait_ge(soft, 1)
                stt_(R0, R0, 0.0, R2, ALU.min, ALU.subtract)
                dve.drain()
                nc.vector.tensor_tensor_scan(R2, R0, R3, 0.0, ALU.add, ALU.add)
                dve.drain()
                tt_(R1, R1, R2, ALU.subtract)
                dve.drain()
                nc.vector.tensor_tensor_scan(R0, R1, R3, 0.0, ALU.max, ALU.add)
                dve.drain()
                tt_(R2, R2, R0, ALU.add).then_inc(am_rows, 1)
                lam = self.cols[:, self.param_at["lambda"][0], self.param_at["lambda"][1]:self.param_at["lambda"][1] + 4]
                stt_(lru_c, lam, -1.0, lam, ALU.mult, ALU.max).then_inc(lam_neg, 1)
                dve.wait_ge(am_t, 1)
                nc.vector.tensor_copy(am, ps[:, 2, 0:32].rearrange("p (t c) -> p t c", t=ST)).then_inc(am_ok, 1)
                dve.drain()
                for h in range(M_HEADS):
                    for j in range(ST):
                        n, k = S - j * P, 4 * h + j
                        if j == 0:
                            dve.wait_ge(mb, h + 1)
                            if h:
                                dve.wait_ge(pv, h)
                        e = prob[:, off[j]:off[j] + n]
                        ts_(e, ps[:, 3, j * P:S], am[:, j, h:h + 1], 0.0, ALU.subtract, ALU.max).then_inc(gap, 1)
                    for j in range(ST):
                        n, k = S - j * P, 4 * h + j
                        e = prob[:, off[j]:off[j] + n]
                        dve.wait_ge(decay, k + 1)
                        tt_(e[:, 0:P], e[:, 0:P], self.c("causal_st"), ALU.mult)
                        dve.wait_ge(score, k + 1)
                        dve.drain()
                        stt_(e, ps[:, 4 + k % 2, 0:n], SCALE, e, ALU.mult, ALU.mult).then_inc(p_ok, 1)
                    dve.wait_ge(pv, h + 1)
                    nc.vector.tensor_copy(A[:, self.MQ + h, :], ps[:, 6, :])
                    nc.vector.tensor_copy(den[:, 4 * h:4 * h + 4], ps[:, 7, 0:4])
                    dve.drain().then_inc(pv_used, 1)
                dve.wait_ge(enm_ok, 1)
                stt_(rcp, den, -1.0, den, ALU.mult, ALU.max)
                dve.drain()
                tt_(rcp, rcp, self.small[:, 148:164], ALU.max)
                dve.drain()
                nc.vector.reciprocal(rcp, rcp)
                dve.drain()
                wide = lambda v: v.unsqueeze(2).to_broadcast([P, 16, P])
                tt_(num, num, wide(rcp), ALU.mult)
                dve.drain()
                nc.vector.tensor_reduce(stat, num, AX.X, ALU.add)
                dve.drain()
                ts_(stat, stat, -1.0 / P, None, ALU.mult)
                dve.drain()
                tt_(num, num, wide(stat), ALU.add).then_inc(cent, 1)
                dve.wait_ge(elam, 1)
                p0, p1, p2, p3 = poly
                ts_(p0, lru_c, 2.0, None, ALU.add)
                dve.drain()
                nc.vector.reciprocal(p0, p0)
                dve.drain()
                tt_(p0, lru_c, p0, ALU.mult)
                dve.drain()
                tt_(p1, p0, p0, ALU.mult)
                ts_(p2, p0, 0.0, 1.0 / 17, ALU.mult, ALU.add)
                dve.drain()
                for d in (15, 13, 11, 9, 7, 5, 3, 1):
                    tt_(p2, p2, p1, ALU.mult)
                    dve.drain()
                    ts_(p2, p2, 1.0 / d, None, ALU.add)
                    dve.drain()
                ts_(p3, lam, -1.0, 0.0, ALU.mult, ALU.max)
                tt_(p2, p2, p0, ALU.mult)
                dve.drain()
                stt_(p2, p2, 2.0, p3, ALU.mult, ALU.add)
                dve.drain()
                ts_(lru_c, p2, 8.0, None, ALU.mult)
                ts_(p0, p2, -8.0, None, ALU.mult)
                dve.drain().then_inc(lru_coef, 1)
                dve.wait_ge(sq_ok, 1)
                nc.vector.tensor_reduce(stat, sqr, AX.X, ALU.add)
                dve.drain()
                ts_(stat, stat, 1.0 / P, EPS, ALU.mult, ALU.add).then_inc(var_ok, 1)
                dve.wait_ge(std_ok, 1)
                nc.vector.reciprocal(stat, stat)
                dve.drain()
                tt_(num, num, wide(stat), ALU.mult)
                dve.drain()
                gate_o = A[:, self.MO:self.MO + 4, :].rearrange("p t (h d) -> p h t d", h=4)
                num4 = A[:, self.MQ:self.MQ + 4, :].rearrange("p h (t d) -> p h t d", t=ST)
                for h in range(M_HEADS):
                    i = tt_(num4[:, h], num4[:, h], gate_o[:, h], ALU.mult)
                dve.drain().then_inc(y_ok, 1)
                for j in range(BT):
                    r, g, t, y = (A[:, x, :] for x in (self.T, self.T + 1, self.T + 2, self.YB + j))
                    dve.wait_ge(rl_ok, 2 * j + 2)
                    tt_(g, g, A[:, self.RX + j, :], ALU.mult)
                    dve.wait_ge(lru_th, j + 1)
                    ts_(y, t, 1.0, None, ALU.add)
                    dve.drain()
                    nc.vector.reciprocal(y, y)
                    dve.drain()
                    stt_(t, t, 2.0, y, ALU.mult, ALU.mult).then_inc(lru_w, 1)
                    dve.wait_ge(lru_sq, j + 1)
                    tt_(g, g, t, ALU.mult)
                    dve.wait_ge(lru_a, j + 1)
                    dve.drain()
                    nc.vector.tensor_tensor_scan(y, r, g, 0.0, ALU.mult, ALU.add)
                    dve.drain()
                    tt_(y, y, A[:, self.RG + j, :], ALU.mult).then_inc(lru_out, 1)

    def stage_gates_attention(self):
        nc, core, ring, ps, A = self.nc, self.core, self.ring, self.ps, self.arena
        u = self.schedule.u0["gates"]
        sem = core.sem
        att, biased, negmax, p_sum, p_t, pt_ok, pt_used, y_ps, y_ok, yt, yt_ok = (
            sem("att"), sem("att_biased"), sem("neg_max"), sem("probs"), sem("probs_t"), sem("probs_t_ok"),
            sem("pv_done"), sem("y_ps"), sem("y_tm"), sem("y_t"), sem("y_t_used"))
        prob = [A[:, self.T, :], A[:, self.T + 1, :]]
        prob_t = [A[:, self.T + 2, :], A[:, self.KI, :]]
        mx = self.small[:, 64:66]
        total = self.small[:, 66:98]
        SC = 64 ** -0.5
        order = [3, 2, 1, 0]

        gate_out = sem("gate_out")
        HEAD_STEPS, TILE_STEPS = 5, 6 * KD

        def gate_steps(pe, first, count):
            for q in range(first, first + count):
                i, rest = divmod(q, 4 * KD)
                b, k = divmod(rest, KD)
                s, t = divmod(b, 2)
                if k == 0 and t == 0:
                    pe.wait_ge(ring.split[s], u + i + 1)
                if k == 0:
                    pe.wait_ge(ring.bank_free[b], u + i)
                w = [v[:, s].rearrange("p (k n) -> p k n", k=KD)[:, k, t * P:t * P + P] for v in (ring.hi, ring.lo)]
                last = three_pass(nc, ps[:, b, :], w, (self.hi[:, k, :], self.lo[:, k, :]), k == 0, k == KD - 1)
                if k == KD - 1:
                    last.then_inc(ring.done[s] if t else ring.tile[s], 1)

        def gate_copies(dve, first, end):
            for q in range(first, end):
                i, b = divmod(q, 4)
                self.wait_tile(dve, u + i, b)
                nc.vector.tensor_copy(A[:, self.GATES + q, :], ps[:, b, :]).then_inc(ring.bank_free[b], 1)
                dve.drain().then_inc(gate_out, 1)

        def copied(n0, h):
            return (n0 * TILE_STEPS + HEAD_STEPS * max(h - 1, 0)) // KD

        def att_pe(pe, n0):
            qt = order[n0]
            n = (qt + 1) * P
            for step in range(A_HEADS + 1):
                if step < A_HEADS:
                    h, c = step, n0 * A_HEADS + step
                    if c:
                        pe.wait_ge(biased, c)
                    r = slice(64 * (h % 2), 64 * (h % 2) + 64)
                    nc.tensor.matmul(ps[:, 4, 0:n], A[r, self.AQ + h // 2, qt * P:qt * P + P],
                                     A[r, self.AK + h // 2, 0:n], start=True, stop=True).then_inc(att, 1)
                if step >= 1:
                    h, c = step - 1, n0 * A_HEADS + step - 1
                    pe.wait_ge(p_sum, c + 1)
                    if c:
                        pe.wait_ge(pt_ok, c)
                    for j in range(qt + 1):
                        last = nc.tensor.transpose(ps[:, 5, j * P:j * P + P], prob[c % 2][:, j * P:j * P + P],
                                                   self.c("ident"))
                    last.then_inc(p_t, 1)
                    gate_steps(pe, n0 * TILE_STEPS + h * HEAD_STEPS, HEAD_STEPS)
                    if h == 0 and n0:
                        pe.wait_ge(y_ok, n0)
                    pe.wait_ge(pt_ok, c + 1)
                    for j in range(qt + 1):
                        last = nc.tensor.matmul(ps[:, 6, h * 64:h * 64 + 64], prob_t[c % 2][:, j * P:j * P + P],
                                                A[:, self.AV + j, h * 64:h * 64 + 64], start=(j == 0),
                                                stop=(j == qt))
                    last.then_inc(pt_used, 1)
            gate_steps(pe, n0 * TILE_STEPS + A_HEADS * HEAD_STEPS, TILE_STEPS - A_HEADS * HEAD_STEPS)
            pe.wait_ge(y_ok, n0 + 1)
            if n0:
                pe.wait_ge(yt_ok, n0)
            for j in range(BT):
                last = nc.tensor.transpose(ps[:, 7, j * P:j * P + P], A[:, self.SC + qt, j * P:j * P + P],
                                           self.c("ident"))
            last.then_inc(yt, 1)

        def att_act(act, n0):
            qt = order[n0]
            n = (qt + 1) * P
            for h in range(A_HEADS):
                c = n0 * A_HEADS + h
                act.wait_ge(negmax, c + 1)
                nc.scalar.activation(prob[c % 2][:, 0:n], prob[c % 2][:, 0:n], ACT.Exp, bias=mx[:, c % 2:c % 2 + 1],
                                     scale=SC, accum_out=total[:, c:c + 1]).then_inc(p_sum, 1)
                act.wait_ge(p_t, c + 1)
                if c >= 2:
                    act.wait_ge(pt_used, c - 1)
                nc.scalar.activation(prob_t[c % 2][:, 0:n], ps[:, 5, 0:n], ACT.Copy).then_inc(pt_ok, 1)
            a, b = copied(n0 - 1, A_HEADS) if n0 else 0, copied(n0, A_HEADS) if n0 < 3 else 24
            act.wait_ge(gate_out, b)
            gates = self.tiles(self.GATES + a, b - a)
            nc.scalar.activation(gates, gates, ACT.Sigmoid)

        def att_dve(dve, n0):
            qt = order[n0]
            n = (qt + 1) * P
            for h in range(A_HEADS):
                c = n0 * A_HEADS + h
                dve.wait_ge(att, c + 1)
                if c >= 2:
                    dve.wait_ge(p_t, c - 1)
                nc.vector.tensor_tensor(prob[c % 2][:, 0:n], ps[:, 4, 0:n], A[:, self.SC + qt, 0:n], ALU.add)\
                    .then_inc(biased, 1)
                dve.drain()
                nc.vector.reduce_max(mx[:, c % 2:c % 2 + 1], prob[c % 2][:, 0:n], AX.X)
                dve.drain()
                nc.vector.tensor_scalar(mx[:, c % 2:c % 2 + 1], mx[:, c % 2:c % 2 + 1], -SC, None, ALU.mult)\
                    .then_inc(negmax, 1)
                gate_copies(dve, copied(n0, h), copied(n0, h + 1))
            dve.wait_ge(pt_used, n0 * A_HEADS + A_HEADS)
            tot = total[:, n0 * A_HEADS:(n0 + 1) * A_HEADS]
            nc.vector.reciprocal(tot, tot)
            dve.drain()
            nc.vector.tensor_tensor(A[:, self.SC + qt, :].rearrange("p (h d) -> p h d", h=A_HEADS),
                                    ps[:, 6, :].rearrange("p (h d) -> p h d", h=A_HEADS),
                                    tot.unsqueeze(2).to_broadcast([P, A_HEADS, 64]), ALU.mult).then_inc(y_ok, 1)
            gate_copies(dve, copied(n0, A_HEADS), copied(n0 + 1, 0))
            dve.wait_ge(yt, n0 + 1)
            nc.vector.tensor_copy(A[:, self.YC:self.YC + 4, qt * P:qt * P + P],
                                  ps[:, 7, :].rearrange("p (j t) -> p j t", j=BT)).then_inc(yt_ok, 1)

        with core.stage() as block:
            @block.sync
            def _(sp):
                self.schedule.run(sp, "load", ["gates"])

            @block.gpsimd
            def _(pool):
                self.schedule.run(pool, "halve", ["gates"])

            @block.tensor
            def _(pe):
                for n0 in range(4):
                    att_pe(pe, n0)

            @block.scalar
            def _(act):
                for n0 in range(4):
                    att_act(act, n0)

            @block.vector
            def _(dve):
                for n0 in range(4):
                    att_dve(dve, n0)

    def stage_ffn_up(self, ada, mod_at):
        sp_n, pe_n, act_n, dve_n = self.norm("norm_ffn")
        adav = ada.rearrange("(k p) n -> p k n", p=P)
        ada_w, acc, sums = self.tiles(0, KD), self.arena[:, 20, :], 8
        ada_in, ada_used, mod_ps = self.core.sem("ada_in"), self.core.sem("ada_used"), self.core.sem("mod_ps")
        c_act = self.small[:, 184:192]
        nc, core, ring, ps, A = self.nc, self.core, self.ring, self.ps, self.arena
        u = self.schedule.u0["up"]
        sem = core.sem
        pad_zero, pad_ok, conv_ok, gelu_ok = sem("pad_zero"), sem("pad_ok"), sem("conv_ok"), sem("gelu_ok")
        pad = self.pad
        g = [A[:, self.T, :], A[:, self.T + 1, :]]
        cb, cr, _ = self.param_at["fconv_w"]
        bb, br, _ = self.param_at["fconv_b"]
        with core.stage() as block:
            @block.sync
            def _(sp):
                self.schedule.run(sp, "load", ["up"])

            @block.gpsimd
            def _(pool):
                self.schedule.run(pool, "halve", ["up"])

            @block.tensor
            def _(pe):
                pe_n(pe)
                self.pe_first(pe, u)
                with pe.Fori(1, 12) as i:
                    self.pe_feature(pe, i + u)
                pe.wait_ge(ada_used, 13)
                for n in range(48):
                    last = nc.tensor.matmul(ps[:, 4, n:n + 1], A[:, sums + n // 4, n % 4 * P:n % 4 * P + P],
                                            self.c("ones")[:, 0:1], start=True, stop=True)
                last.then_inc(mod_ps, 1)

            @block.scalar
            def _(act):
                act_n(act)
                act.wait_ge(pad_zero, 1)
                with act.Fori(0, 12) as i:
                    act.wait_ge(ada_used, i + 1)
                    act.dma_start(ada_w, adav[:, :, bass.ds(i * 512, 512)]).then_inc(ada_in, 16)
                    for t in (0, 1):
                        self.wait_tile(act, i + u, t)
                        nc.scalar.activation(pad[t][:, 3:3 + S], ps[:, t, :], ACT.Copy)\
                            .then_inc(ring.bank_free[t], 1)
                        act.drain().then_inc(pad_ok, 1)
                    for t in (0, 1):
                        act.wait_ge(conv_ok, i * 2 + (t + 1))
                        nc.scalar.activation(g[t], g[t], ACT.Gelu_apprx_tanh).then_inc(gelu_ok, 1)

            @block.vector
            def _(dve):
                dve.sem_inc(ada_used, 1)
                dve_n(dve)
                for b in (0, 1):
                    nc.vector.memset(pad[b][:, 0:3], 0.0)
                dve.drain().then_inc(pad_zero, 1)
                with dve.Fori(0, 12) as i:
                    for t in (0, 1):
                        dve.drain()
                        dve.wait_ge(pad_ok, i * 2 + (t + 1))
                        w = [self.cols[:, cb, bass.ds(i * 2 + (cr + 24 * k + t), 1)] for k in range(3)]
                        bias = self.cols[:, bb, bass.ds(i * 2 + (br + t), 1)]
                        nc.vector.tensor_scalar(g[t], pad[t][:, 1:1 + S], w[0], bias, ALU.mult, ALU.add)
                        for k in (1, 2):
                            dve.drain()
                            ins = nc.vector.scalar_tensor_tensor(g[t], pad[t][:, 1 + k:1 + k + S], w[k], g[t],
                                                                 ALU.mult, ALU.add)
                        ins.then_inc(conv_ok, 1)
                    for t in (0, 1):
                        dve.wait_ge(gelu_ok, i * 2 + (t + 1))
                        self.wait_tile(dve, i + u, 2 + t)
                        dst = A[:, bass.ds(i * 2 + (self.HID + t), 1), :].rearrange("p a n -> p (a n)")
                        nc.vector.tensor_tensor(dst, ps[:, 2 + t, :], g[t], ALU.mult)\
                            .then_inc(ring.bank_free[2 + t], 1)
                    dve.wait_ge(ada_in, i * 16 + 16)
                    nc.vector.tensor_scalar(acc, ada_w[:, 0, :], c_act[:, 0:1], None, ALU.mult)
                    for k in range(1, KD):
                        dst = acc if k < KD - 1 else \
                            A[:, bass.ds(i + sums, 1), :].rearrange("p a n -> p (a n)")
                        dve.drain()
                        ins = nc.vector.scalar_tensor_tensor(dst, ada_w[:, k, :], c_act[:, k:k + 1], acc,
                                                             ALU.mult, ALU.add)
                    ins.then_inc(ada_used, 1)
                dve.wait_ge(mod_ps, 1)
                nc.vector.tensor_copy(mod_at, ps[:, 4, 0:48])



class Second(Kernel):

    R, K, V, B, KK, G, GG, YB = 0, 4, 8, 12, 16, 20, 24, 28
    VF, BV = 32, 36
    LORA, RESET, LW, POOLW = 44, 47, 48, 51
    TMP = 40
    KB_TM, V_TM, BB_TM = 32, 40, 44
    HID = 28

    def __init__(self, first):
        self.nc, self.core, self.ring, self.x = first.nc, first.core, first.ring, first.x
        self.hi, self.lo, self.const = first.hi, first.lo, first.const
        self.rows, self.cols, self.small, self.arena = first.rows, first.cols, first.small, first.arena
        self.pad, self.ps = first.pad, first.ps
        self.mod = self.small[:, 64:112]

    def make_schedule(self, w_in, v_down, proj_a, proj_b, w_out, gu, down):
        ring = self.ring
        raw = [ring.raw[:, s].rearrange("p (k n) -> p k n", k=8) for s in (0, 1)]
        raw4 = [ring.raw[:, s].rearrange("p (k n) -> p k n", k=4) for s in (0, 1)]
        raw2 = [ring.raw[:, s].rearrange("p (k n) -> p k n", k=2) for s in (0, 1)]
        win, vd, guv = (w.rearrange("(k p) n -> p k n", p=P) for w in (w_in, v_down, gu))

        def columns(v, first, other=SLOT, step=512):
            return lambda i, s: [(raw[s], v[:, :, bass.ds(i * step + first + s * other, SLOT)])]

        def lora(i, s):
            if s == 0:
                return [(raw[0], win[:, :, C2_LORA:C2_LORA + SLOT])]
            return [(raw[1][:, :, 0:32], win[:, :, C2_GL1:C2_GL1 + 32]), (raw[1][:, :, 32:64], vd),
                    (raw[1][:, :, 64:SLOT], win[:, :, C2_POOL:C2_POOL + SLOT - 64])]

        def proj(w):
            v = w.rearrange("(k p) n -> p k n", p=P)
            return lambda i, s: [(raw4[s], v[:, :, s * 512:(s + 1) * 512])]

        def rows_of(w, base=0):
            v = w.rearrange("(q k p) n -> q p k n", p=P, k=2)
            return lambda i, s: [(raw2[s], v[2 * i + s + base])]

        whole = lambda b: b
        self.schedule = Schedule(ring, [
            Section("lora", 1, lora, dmas=(1, 3)),
            Section("rkv", 3, columns(win, C2_R)),
            Section("pool", 1, columns(win, C2_POOL)),
            Section("gates", 4, columns(win, C2_GATE)),
            Section("branch", 1, proj(proj_a)), Section("branch_b", 1, proj(proj_b)),
            Section("w_out", 2, rows_of(w_out)),
            Section("gu", 11, columns(guv, 0, D_FF2, SLOT)),
            Section("down", 5, rows_of(down)),
            Section("down_last", 1, lambda i, s: [] if s else rows_of(down, 10)(0, 0),
                    view=(whole, None), dmas=(1, 0)),
        ])

    def stage_inputs(self, pool_w, params, mod_all):
        sp_n, pe_n, act_n, dve_n = self.norm("norm1", scale=self.mod[:, 8:16], shift=lambda j: self.mod[:, j:j + 1],
                                             params=params, mod_of=(mod_all, "ada_b"))
        nc, core, ring, ps, A = self.nc, self.core, self.ring, self.ps, self.arena
        u = self.schedule.u0
        sem = core.sem
        pad, pad_zero, pad_ok, shift_ok = self.pad, sem("pad_zero"), sem("pad_ok"), sem("shift_ok")
        poolw_in, pooled_ok, pool_prod, pool_read = sem("pool_w_in"), sem("pooled"), sem("pool_product"), sem("pool_read")
        tmp = [A[:, self.TMP, :], A[:, self.TMP + 1, :]]
        wide = A[:, 42:44, :].rearrange("p a n -> p (a n)")[:, 0:S + 16]
        pw = A[:, self.POOLW, :].rearrange("p (g d) -> p g d", g=4)
        names = ["lora", "rkv", "pool"]
        W = 16
        mu_buf, mu_row, _ = self.param_at["mu"]

        def shift_act(act, n, u_, b):
            self.wait_tile(act, u_, b)
            act.wait_ge(shift_ok, n)
            nc.scalar.activation(pad[b % 2][:, W:W + S], ps[:, b, :], ACT.Copy).then_inc(ring.bank_free[b], 1)
            act.drain().then_inc(pad_ok, 1)

        def shift_dve(dve, n, b, mu, dst):
            dve.drain()
            dve.wait_ge(pad_ok, n)
            z, before = pad[b % 2][:, W:W + S], pad[b % 2][:, W - 1:W - 1 + S]
            nc.vector.tensor_tensor(tmp[b % 2], before, z, ALU.subtract)
            dve.drain()
            nc.vector.scalar_tensor_tensor(dst, tmp[b % 2], mu, z, ALU.mult, ALU.add).then_inc(shift_ok, 1)

        def pool_out(act, g):
            act.wait_ge(pool_prod, g + 1)
            nc.scalar.activation(A[:, self.YB + g, :], ps[:, 4 + g % 2, :], ACT.Copy,
                                 scale=self.col("pool_scale", g)).then_inc(pool_read, 1)

        with core.stage() as block:
            @block.sync
            def _(sp):
                sp_n(sp)
                self.schedule._pair(sp, self.schedule.sections[0], 0, "load")
                self.schedule.run(sp, "load", names)
                sp.wait_ge(self.norm_lo, KD)
                sp.dma_start(pw, pool_w.rearrange("g c d -> c g d")).then_inc(poolw_in, 16)

            @block.gpsimd
            def _(pool):
                self.schedule._pair(pool, self.schedule.sections[0], 0, "halve")
                self.schedule.run(pool, "halve", names)

            @block.tensor
            def _(pe):
                pe_n(pe)
                self.pe_first(pe, u["lora"])
                with pe.Fori(0, 3) as i:
                    self.pe_feature(pe, i + u["rkv"])
                self.pe_feature(pe, u["pool"])
                pe.wait_ge(poolw_in, 16)
                for g in range(4):
                    pe.wait_ge(pooled_ok, g + 1)
                    if g >= 2:
                        pe.wait_ge(pool_read, g - 1)
                    nc.tensor.matmul(ps[:, 4 + g % 2, :], pw[:, g, :], A[:, self.TMP + g % 2, :],
                                     start=True, stop=True).then_inc(pool_prod, 1)

            @block.scalar
            def _(act):
                act_n(act)
                act.wait_ge(pad_zero, 1)
                for b in range(3):
                    shift_act(act, b + 1, u["lora"], b)
                self.wait_tile(act, u["lora"], 3)
                act.sem_inc(ring.bank_free[3], 1)
                with act.Fori(0, 3) as i:
                    for b in range(4):
                        self.wait_tile(act, i + u["rkv"], b)
                        act.wait_ge(shift_ok, i * 4 + (b + 5))
                        nc.scalar.activation(pad[b % 2][:, W:W + S], ps[:, b, :], ACT.Copy)\
                            .then_inc(ring.bank_free[b], 1)
                        act.drain().then_inc(pad_ok, 1)
                for g in range(4):
                    self.wait_tile(act, u["pool"], g)
                    act.wait_ge(shift_ok, 17)
                    if g:
                        act.wait_ge(pooled_ok, g)
                    nc.scalar.activation(pad[0][:, W:W + S], ps[:, g, :], ACT.Copy).then_inc(ring.bank_free[g], 1)
                    act.drain().then_inc(pad_ok, 1)
                    if g:
                        pool_out(act, g - 1)
                pool_out(act, 3)

            @block.vector
            def _(dve):
                dve_n(dve)
                nc.vector.memset(pad[0][:, 0:W], 0.0)
                nc.vector.memset(pad[1][:, 0:W], 0.0)
                nc.vector.memset(wide[:, 0:W], 0.0)
                dve.sem_inc(shift_ok, 2)
                dve.drain().then_inc(pad_zero, 1)
                for b, name in enumerate(("mu_l0", "mu_l1", "mu_l2")):
                    shift_dve(dve, b + 1, b, self.col(name), A[:, self.LORA + b, :])
                with dve.Fori(0, 3) as i:
                    for b in range(4):
                        dst = A[:, bass.ds(i * 4 + (self.R + b), 1), :].rearrange("p a n -> p (a n)")
                        mu = self.cols[:, mu_buf, bass.ds(i * 4 + (mu_row + b), 1)]
                        shift_dve(dve, i * 4 + (b + 4), b, mu, dst)
                for g in range(4):
                    dve.drain()
                    dve.wait_ge(pad_ok, 16 + g)
                    out = A[:, self.TMP + g % 2, :]
                    if g >= 2:
                        dve.wait_ge(pool_prod, g - 1)
                    src, bufs = pad[0], [pad[1], wide]
                    for step in range(g + 1):
                        dst = bufs[step % 2]
                        nc.vector.tensor_tensor(dst[:, W:W + S], src[:, W:W + S],
                                                src[:, W - 2 ** step:W - 2 ** step + S], ALU.add)
                        dve.drain()
                        src = dst
                    ic = self.c("inv_count")[:, 16 * g:16 * g + 16]
                    nc.vector.tensor_tensor(out[:, 0:16], src[:, W:W + 16], ic, ALU.mult)
                    dve.drain()
                    nc.vector.tensor_tensor(out[:, 0:16], out[:, 0:16], pad[0][:, W:W + 16], ALU.subtract)
                    nc.vector.scalar_tensor_tensor(out[:, 16:S], src[:, W + 16:W + S], 1.0 / 2 ** (g + 1),
                                                   pad[0][:, W + 16:W + S], ALU.mult, ALU.subtract)
                    dve.drain().then_inc(pooled_ok, 1)

    def stage_prepare(self, w_up, a_up, v_up, g_up, v_first):
        nc, core, ps, A = self.nc, self.core, self.ps, self.arena
        sem = core.sem
        w_in_s, vf_in, vf_ok, act0 = sem("lora_w_in"), sem("v_first_in"), sem("v_first_ok"), sem("lora_act")
        lora_ps, dec, aa, gg, vv = sem("lora_ps"), sem("decay_sig"), sem("a_sig"), sem("g_out"), sem("v_sig")
        sq_ok, ss, root, rk_ok, bonus, used = (sem("key_sq"), sem("key_ss"), sem("key_root"), sem("rk"),
                                               sem("bonus"), sem("bonus_used"))
        cum, exps, tmp_free = sem("cum"), sem("exps"), sem("tmp_free")
        WUA, GU0, GUV = (A[:, self.LW + j, :] for j in range(3))
        L0, L1, L2 = (A[:, self.LORA + j, :] for j in range(3))
        T = [A[:, self.TMP + j, :] for j in range(4)]
        reset = A[:, self.RESET, :]
        X0 = A[:, 51, :]
        egl = self.small[:, 0:32]
        later = self.small[:, 299:300]
        EM = -math.exp(-0.5)
        with core.stage() as block:
            @block.sync
            def _(sp):
                sp.dma_start(WUA[0:64, :], w_up).then_inc(w_in_s, 16)
                sp.dma_start(WUA[64:128, :], a_up).then_inc(w_in_s, 16)
                sp.dma_start(GU0, g_up[0:128, :]).then_inc(w_in_s, 16)
                sp.dma_start(GUV[0:32, :], g_up[128:160, :]).then_inc(w_in_s, 16)
                sp.dma_start(GUV[32:64, :], v_up).then_inc(w_in_s, 16)
                sp.dma_start(self.tiles(self.VF, 4), v_first).then_inc(vf_in, 16)
                sp.wait_ge(vf_ok, 4)
                sp.dma_start(v_first, self.tiles(self.VF, 4)).then_inc(vf_in, 16)
                sp.wait_ge(vf_in, 32)

            @block.tensor
            def _(pe):
                pe.wait_ge(w_in_s, 80)
                pe.wait_ge(act0, 1)
                for j in range(4):
                    if j:
                        pe.wait_ge(used, j)
                    c = slice(j * P, j * P + P)
                    nc.tensor.matmul(ps[:, 0, :], WUA[0:64, c], L0[0:64, :], start=True, stop=True)
                    nc.tensor.matmul(ps[:, 1, :], WUA[64:128, c], L0[64:128, :], start=True, stop=True)
                    nc.tensor.matmul(ps[:, 2, :], GU0[:, c], L1, start=True, stop=False)
                    nc.tensor.matmul(ps[:, 2, :], GUV[0:32, c], L2[0:32, :], start=False, stop=True)
                    nc.tensor.matmul(ps[:, 3, :], GUV[32:64, c], L2[32:64, :], start=True, stop=True)\
                        .then_inc(lora_ps, 1)
                    pe.wait_ge(sq_ok, j + 1)
                    nc.tensor.matmul(ps[:, 4, :], self.c("blockones"), T[2], start=True, stop=True)\
                        .then_inc(ss, 1)
                    pe.wait_ge(rk_ok, j + 1)
                    nc.tensor.matmul(ps[:, 5, :], self.c("blockones"), T[3], start=True, stop=True)\
                        .then_inc(bonus, 1)

            @block.scalar
            def _(act):
                nc.scalar.activation(L0[0:64, :], L0[0:64, :], ACT.Tanh)
                nc.scalar.activation(L1, L1, ACT.Sigmoid)
                nc.scalar.activation(L2[0:32, :], L2[0:32, :], ACT.Sigmoid)
                act.drain().then_inc(act0, 1)
                for j in range(4):
                    act.wait_ge(lora_ps, j + 1)
                    if j:
                        act.wait_ge(used, j)
                    nc.scalar.activation(T[0], ps[:, 0, :], ACT.Sigmoid, bias=self.col("w0", j)).then_inc(dec, 1)
                    nc.scalar.activation(A[:, self.B + j, :], ps[:, 1, :], ACT.Sigmoid, bias=self.col("a0", j))\
                        .then_inc(aa, 1)
                    nc.scalar.activation(A[:, self.GG + j, :], ps[:, 2, :], ACT.Copy).then_inc(gg, 1)
                    nc.scalar.activation(T[1], ps[:, 3, :], ACT.Sigmoid, bias=self.col("v0", j)).then_inc(vv, 1)
                    act.wait_ge(ss, j + 1)
                    nc.scalar.activation(T[2], ps[:, 4, :], ACT.Sqrt).then_inc(root, 1)
                    act.wait_ge(cum, j + 1)
                    nc.scalar.activation(T[0], A[:, self.G + j, :], ACT.Exp)
                    nc.scalar.activation(T[1], A[:, self.G + j, :], ACT.Exp, scale=-1.0)
                    act.drain().then_inc(exps, 1)

            @block.vector
            def _(dve):
                ts_, tt_, stt_ = nc.vector.tensor_scalar, nc.vector.tensor_tensor, nc.vector.scalar_tensor_tensor
                nc.vector.memset(reset, 1.0)
                dve.drain()
                nc.vector.memset(reset.rearrange("p (c t) -> p c t", t=CH)[:, :, 0:1], 0.0)
                dve.drain()
                dve.wait_ge(vf_in, 16)
                for j in range(4):
                    r, kx, v, b, kk, g, vf = (A[:, x + j, :] for x in (self.R, self.K, self.V, self.B, self.KK,
                                                                       self.G, self.VF))
                    ts_(kk, kx, self.col("k_k", j), None, ALU.mult)
                    dve.drain()
                    tt_(T[2], kk, kk, ALU.mult).then_inc(sq_ok, 1)
                    dve.wait_ge(dec, j + 1)
                    ts_(T[0], T[0], EM, None, ALU.mult)
                    dve.drain()
                    nc.vector.tensor_tensor_scan(g, reset, T[0], 0.0, ALU.mult, ALU.add)
                    tt_(X0, vf, v, ALU.subtract)
                    dve.drain()
                    ts_(X0, X0, later, None, ALU.mult)
                    dve.drain()
                    tt_(vf, v, X0, ALU.add).then_inc(vf_ok, 1)
                    dve.wait_ge(vv, j + 1)
                    tt_(X0, X0, T[1], ALU.mult)
                    dve.drain()
                    tt_(v, v, X0, ALU.add)
                    dve.drain().then_inc(cum, 1)
                    dve.wait_ge(aa, j + 1)
                    ts_(X0, b, 1.0, self.col("k_a", j), ALU.subtract, ALU.mult)
                    dve.drain()
                    stt_(kx, X0, 1.0, kx, ALU.add, ALU.mult)
                    dve.drain()
                    stt_(T[3], r, self.col("r_k", j), kx, ALU.mult, ALU.mult).then_inc(rk_ok, 1)
                    dve.wait_ge(root, j + 1)
                    ts_(T[2], T[2], 1e-12, None, ALU.max)
                    dve.drain()
                    nc.vector.reciprocal(T[2], T[2])
                    dve.drain()
                    tt_(kk, kk, T[2], ALU.mult)
                    dve.drain()
                    tt_(b, b, kk, ALU.mult)
                    dve.wait_ge(bonus, j + 1)
                    tt_(A[:, self.BV + j, :], ps[:, 5, :], v, ALU.mult)
                    dve.wait_ge(exps, j + 1)
                    dve.drain()
                    tt_(r, r, T[0], ALU.mult)
                    k3, e3 = (y.rearrange("p (c t) -> p c t", t=CH) for y in (kk, T[0]))
                    tt_(k3[:, :, 1:CH], k3[:, :, 1:CH], e3[:, :, 0:CH - 1], ALU.mult)
                    tt_(kx, kx, T[1], ALU.mult)
                    tt_(b, b, T[1], ALU.mult)
                    nc.vector.tensor_copy(egl[:, 8 * j:8 * j + 8].unsqueeze(2), e3[:, :, CH - 1:CH])
                    dve.drain().then_inc(used, 1)
                nc.vector.memset(later, 1.0)

    def halves(self, h):
        return slice(64 * h, 64 * h + 64)

    def stage_token_major(self):
        nc, core, ps, A = self.nc, self.core, self.ps, self.arena
        t_ok, t_used = core.sem("turned"), core.sem("turned_used")
        jobs = [(src, dst, g) for src, dst in ((self.V, self.V_TM), (self.K, self.KB_TM), (self.B, self.BB_TM))
                for g in range(4)]
        with core.stage() as block:
            @block.tensor
            def _(pe):
                for n, (src, _, g) in enumerate(jobs):
                    if n >= 4:
                        pe.wait_ge(t_used, n - 3)
                    for cc in (0, 1):
                        for pr in range(NP):
                            for h in (0, 1):
                                q = self.halves(h)
                                col = (cc * NP + pr) * CH
                                tok = (2 * g + cc) * CH
                                last = nc.tensor.matmul(ps[q, n % 4, col:col + CH], A[q, src + pr, tok:tok + CH],
                                                        self.c("ident")[q, q], start=True, stop=True)
                    last.then_inc(t_ok, 1)

            @block.scalar
            def _(act):
                for n, (_, dst, g) in enumerate(jobs):
                    act.wait_ge(t_ok, n + 1)
                    nc.scalar.activation(A[:, dst + g, :], ps[:, n % 4, :], ACT.Copy,
                                         scale=-1.0 if dst == self.BB_TM else 1.0).then_inc(t_used, 1)

    def stage_scan(self):
        nc, core, ps, A = self.nc, self.core, self.ps, self.arena
        sem = core.sem
        AT, W = A[:, 48, :], A[:, 51, :]
        XX = [A[:, 49 + cc, :] for cc in (0, 1)]
        AKT, PKT, PBT = (A[:, 8 + j, :] for j in range(3))
        state, U = ([A[:, t, i * 256:i * 256 + 256] for i in (0, 1)] for t in (11, 20))
        rhs = A[:, 21, 0:256]
        w_bank, x_bank = (5, 7), (6, 1)
        egl = self.small[:, 0:32].rearrange("p (j c) -> p j c", c=NCH)
        prod, prod_used = sem("products"), sem("products_read")
        w_ps, w_ok, x_ps, x_ok = sem("w_ps"), sem("w_ok"), sem("x_ps"), sem("x_ok")
        r_ps, r_ok, u_ps, u_ok, y_ps, s_ps, s_ok, y_used = (sem("rhs_ps"), sem("rhs_ok"), sem("u_ps"), sem("u_ok"),
                                                            sem("y_ps"), sem("state_ps"), sem("state_ok"),
                                                            sem("y_read"))
        wide = lambda m: m.unsqueeze(1).to_broadcast([P, 8, CH])
        as3 = lambda v: v.rearrange("p (u n) -> p u n", n=CH)
        LEVELS = (2, 4, 8, 16, 32)
        units = [(cc, pr, h) for cc in (0, 1) for pr in range(NP) for h in (0, 1)]
        pairs = [(pr, h) for pr in range(NP) for h in (0, 1)]
        cols = lambda cc, pr: slice((cc * NP + pr) * CH, (cc * NP + pr) * CH + CH)

        def y_pairs(g, cc, pr):
            tok = slice((2 * g + cc) * CH, (2 * g + cc) * CH + CH)
            for h in (0, 1):
                q, col, o, yb = self.halves(h), cols(cc, pr), slice(pr * CH, pr * CH + CH), 3 + cc
                nc.tensor.matmul(ps[q, yb, o], A[q, self.R + pr, tok], state[cc][q, o], start=True, stop=False)
                nc.tensor.matmul(ps[q, yb, o], PKT[q, col], A[q, self.V_TM + g, col], start=False, stop=False)
                last = nc.tensor.matmul(ps[q, yb, o], PBT[q, col], U[cc][q, o], start=False, stop=True)
            return last

        with core.stage() as block:
            @block.tensor
            def _(pe):
                for g in range(4):
                    if g:
                        pe.wait_ge(y_used, 2 * g)
                    for cc, pr, h in units:
                        q, col = self.halves(h), (cc * NP + pr) * CH
                        tok = slice((2 * g + cc) * CH, (2 * g + cc) * CH + CH)
                        r, k, b, kk = (A[q, x + pr, tok] for x in (self.R, self.K, self.B, self.KK))
                        for bank, lhs, rhs_ in ((0, b, kk), (1, kk, b), (2, k, kk), (3, k, r), (4, b, r)):
                            last = nc.tensor.matmul(ps[q, bank, col:col + CH], lhs, rhs_, start=True, stop=True)
                    last.then_inc(prod, 1)
                    for n, lv in enumerate(LEVELS):
                        for cc in (0, 1):
                            pe.wait_ge(x_ok, 12 * g + 2 * n + cc + 1)
                            for pr, h in pairs:
                                q, col, o = self.halves(h), cols(cc, pr), slice(pr * CH, pr * CH + CH)
                                last = nc.tensor.matmul(ps[q, w_bank[cc], o], AT[q, col], XX[cc][q, o],
                                                        start=True, stop=True)
                            last.then_inc(w_ps, 1)
                        for cc in (0, 1):
                            pe.wait_ge(w_ok, 10 * g + 2 * n + cc + 1)
                            for pr, h in pairs:
                                q, col, o = self.halves(h), cols(cc, pr), slice(pr * CH, pr * CH + CH)
                                ot = slice(256 + pr * CH, 256 + pr * CH + CH)
                                nc.tensor.matmul(ps[q, x_bank[cc], o], XX[cc][q, ot], W[q, col],
                                                 start=True, stop=True)
                                last = nc.tensor.matmul(ps[q, x_bank[cc], ot], W[q, col], XX[cc][q, ot],
                                                        start=True, stop=True)
                            last.then_inc(x_ps, 1)
                    pe.wait_ge(x_ok, 12 * g + 12)
                    pe.wait_ge(prod_used, g + 1)
                    for cc in (0, 1):
                        c = 2 * g + cc
                        tok = slice(c * CH, c * CH + CH)
                        pe.wait_ge(s_ok, c + 1)
                        for pr, h in pairs:
                            q, col, o = self.halves(h), cols(cc, pr), slice(pr * CH, pr * CH + CH)
                            nc.tensor.matmul(ps[q, 5, o], A[q, self.KK + pr, tok], state[cc][q, o],
                                             start=True, stop=False)
                            last = nc.tensor.matmul(ps[q, 5, o], AKT[q, col], A[q, self.V_TM + g, col],
                                                    start=False, stop=True)
                        last.then_inc(r_ps, 1)
                        if cc:
                            y_pairs(g, 0, 2)
                        pe.wait_ge(r_ok, c + 1)
                        for pr, h in pairs:
                            q, o = self.halves(h), slice(pr * CH, pr * CH + CH)
                            last = nc.tensor.matmul(ps[q, 6, o], XX[cc][q, 256 + pr * CH:256 + pr * CH + CH],
                                                    rhs[q, o], start=True, stop=True)
                        last.then_inc(u_ps, 1)
                        if cc:
                            y_pairs(g, 0, 3).then_inc(y_ps, 1)
                        pe.wait_ge(u_ok, c + 1)
                        for pr, h in pairs:
                            q, col, o = self.halves(h), cols(cc, pr), slice(pr * CH, pr * CH + CH)
                            nc.tensor.matmul(ps[q, 7, o], A[q, self.KB_TM + g, col], A[q, self.V_TM + g, col],
                                             start=True, stop=False)
                            last = nc.tensor.matmul(ps[q, 7, o], A[q, self.BB_TM + g, col], U[cc][q, o],
                                                    start=False, stop=True)
                        last.then_inc(s_ps, 1)
                        for pr in range(NP if cc else 2):
                            last = y_pairs(g, cc, pr)
                        if cc:
                            last.then_inc(y_ps, 1)

            @block.scalar
            def _(act):
                for g in range(4):
                    for cc in (0, 1):
                        c = 2 * g + cc
                        act.wait_ge(y_ps, c + 1)
                        nc.scalar.activation(A[:, self.KB_TM + g, cc * 256:cc * 256 + 256], ps[:, 3 + cc, 0:256],
                                             ACT.Copy).then_inc(y_used, 1)

            @block.vector
            def _(dve):
                tt_, stt_ = nc.vector.tensor_tensor, nc.vector.scalar_tensor_tensor
                half = lambda v, cc: v.rearrange("p (c n) -> p c n", c=2)[:, cc, :]
                nc.vector.memset(state[0], 0.0).then_inc(s_ok, 1)
                for g in range(4):
                    dve.wait_ge(prod, g + 1)
                    if g:
                        dve.wait_ge(y_ps, 2 * g)
                    dve.drain()
                    tt_(as3(AT), as3(ps[:, 0, :]), wide(self.c("upper")), ALU.mult)
                    level1 = self.c("level1").unsqueeze(1).to_broadcast([P, NP, CH])
                    level1t = self.c("levelT1").unsqueeze(1).to_broadcast([P, NP, CH])
                    for cc in (0, 1):
                        tt_(as3(half(XX[cc], 0)), as3(half(ps[:, 1, :], cc)), level1, ALU.mult)
                        tt_(as3(half(XX[cc], 1)), as3(half(ps[:, 0, :], cc)), level1t, ALU.mult)
                        dve.drain()
                        tt_(as3(XX[cc]), wide(self.c("ident2")), as3(XX[cc]), ALU.subtract)
                        dve.drain().then_inc(x_ok, 1)
                    tt_(as3(AKT), as3(ps[:, 2, :]), wide(self.c("upper")), ALU.mult)
                    tt_(as3(PKT), as3(ps[:, 3, :]), wide(self.c("upper_eq")), ALU.mult)
                    stt_(as3(PBT), as3(ps[:, 4, :]), -1.0, wide(self.c("upper_eq")), ALU.mult, ALU.mult)
                    dve.drain().then_inc(prod_used, 1)
                    for n, lv in enumerate(LEVELS):
                        level = self.c(f"level{lv}").unsqueeze(1).to_broadcast([P, NP, CH])
                        for cc in (0, 1):
                            dve.wait_ge(w_ps, 10 * g + 2 * n + cc + 1)
                            tt_(as3(half(W, cc)), as3(ps[:, w_bank[cc], 0:256]), level, ALU.mult).then_inc(w_ok, 1)
                        for cc in (0, 1):
                            dve.wait_ge(x_ps, 10 * g + 2 * n + cc + 1)
                            tt_(XX[cc], XX[cc], ps[:, x_bank[cc], :], ALU.subtract)
                            dve.drain().then_inc(x_ok, 1)
                    for cc in (0, 1):
                        c = 2 * g + cc
                        old, new = state[cc], state[1 - cc]
                        dve.wait_ge(r_ps, c + 1)
                        nc.vector.tensor_copy(rhs, ps[:, 5, 0:256]).then_inc(r_ok, 1)
                        dve.wait_ge(u_ps, c + 1)
                        nc.vector.tensor_copy(U[cc], ps[:, 6, 0:256]).then_inc(u_ok, 1)
                        dve.wait_ge(s_ps, c + 1)
                        tt_(new, old, ps[:, 7, 0:256], ALU.add)
                        dve.drain()
                        tt_(as3(new), as3(new), egl[:, :, c:c + 1].to_broadcast([P, NP, CH]), ALU.mult)\
                            .then_inc(s_ok, 1)

    def stage_gates_output(self):
        nc, core, ring, ps, A = self.nc, self.core, self.ring, self.ps, self.arena
        u = self.schedule.u0["gates"]
        sem = core.sem
        cent, sq_ok, var_ok, root, y_ok, yt, y_out = (sem("centred"), sem("squared"), sem("var"), sem("std"),
                                                      sem("y_tm"), sem("y_t"), sem("y_affine"))
        y = self.tiles(self.KB_TM, 4).rearrange("p g (u n) -> p (g u) n", n=CH)
        sq = self.tiles(self.TMP, 4).rearrange("p g (u n) -> p (g u) n", n=CH)
        stat = self.small[:, 32:64]
        wide = lambda v: v.unsqueeze(2).to_broadcast([P, 32, CH])
        with core.stage() as block:
            @block.sync
            def _(sp):
                self.schedule.run(sp, "load", ["gates"])

            @block.gpsimd
            def _(pool):
                self.schedule.run(pool, "halve", ["gates"])

            @block.tensor
            def _(pe):
                for i in range(3):
                    self.pe_feature(pe, u + i)
                pe.wait_ge(y_ok, 1)
                for pr in range(NP):
                    for c in range(NCH):
                        for h in (0, 1):
                            q = self.halves(h)
                            col = ((c % 2) * NP + pr) * CH
                            last = nc.tensor.matmul(ps[q, 4 + pr, c * CH:c * CH + CH],
                                                    A[q, self.KB_TM + c // 2, col:col + CH],
                                                    self.c("ident")[q, q], start=True, stop=True)
                    last.then_inc(yt, 1)
                self.pe_feature(pe, u + 3)

            @block.scalar
            def _(act):
                def gates(i):
                    for b in range(4):
                        self.wait_tile(act, u + i, b)
                        nc.scalar.activation(A[:, self.K + 4 * i + b, :], ps[:, b, :], ACT.Sigmoid)\
                            .then_inc(ring.bank_free[b], 1)
                act.wait_ge(cent, 1)
                nc.scalar.activation(sq, y, ACT.Square).then_inc(sq_ok, 1)
                gates(0)
                act.wait_ge(var_ok, 1)
                nc.scalar.activation(stat, stat, ACT.Sqrt).then_inc(root, 1)
                gates(1)
                gates(2)
                for pr in range(NP):
                    act.wait_ge(yt, pr + 1)
                    nc.scalar.activation(A[:, self.R + pr, :], ps[:, 4 + pr, :], ACT.Identity,
                                         scale=self.col("lnx_g", pr), bias=self.col("lnx_b", pr)).then_inc(y_out, 1)
                gates(3)

            @block.vector
            def _(dve):
                tt_, ts_ = nc.vector.tensor_tensor, nc.vector.tensor_scalar
                nc.vector.tensor_reduce(stat, y, AX.X, ALU.add)
                dve.drain()
                ts_(stat, stat, -1.0 / CH, None, ALU.mult)
                dve.drain()
                tt_(y, y, wide(stat), ALU.add).then_inc(cent, 1)
                dve.wait_ge(sq_ok, 1)
                nc.vector.tensor_reduce(stat, sq, AX.X, ALU.add)
                dve.drain()
                ts_(stat, stat, 1.0 / CH, EPS_GN, ALU.mult, ALU.add).then_inc(var_ok, 1)
                dve.wait_ge(root, 1)
                nc.vector.reciprocal(stat, stat)
                dve.drain()
                tt_(y, y, wide(stat), ALU.mult).then_inc(y_ok, 1)
                for pr in range(NP):
                    dst = A[:, self.R + pr, :]
                    dve.wait_ge(y_out, pr + 1)
                    tt_(dst, dst, A[:, self.BV + pr, :], ALU.add)
                    dve.drain()
                    tt_(dst, dst, A[:, self.GG + pr, :], ALU.mult)

    def stage_gate_up(self):
        sp_n, pe_n, act_n, dve_n = self.norm("norm2", scale=self.mod[:, 32:40],
                                             shift=lambda j: self.mod[:, 24 + j:25 + j])
        nc, core, ring, ps, A = self.nc, self.core, self.ring, self.ps, self.arena
        u = self.schedule.u0["gu"]
        silu_ok, used = core.sem("silu_ok"), core.sem("silu_used")
        g = [A[:, 0, :], A[:, 1, :]]
        with core.stage() as block:
            @block.sync
            def _(sp):
                self.schedule.run(sp, "load", ["gu"])

            @block.gpsimd
            def _(pool):
                self.schedule.run(pool, "halve", ["gu"])

            @block.tensor
            def _(pe):
                pe_n(pe)
                self.pe_first(pe, u)
                with pe.Fori(1, 11) as i:
                    self.pe_feature(pe, i + u)

            @block.scalar
            def _(act):
                act_n(act)
                with act.Fori(0, 11) as i:
                    for t in (0, 1):
                        self.wait_tile(act, i + u, t)
                        act.wait_ge(used, i * 2 + (t + 1))
                        nc.scalar.activation(g[t], ps[:, t, :], ACT.Silu).then_inc(silu_ok, 1)

            @block.vector
            def _(dve):
                dve_n(dve)
                dve.sem_inc(used, 2)
                with dve.Fori(0, 11) as i:
                    for t in (0, 1):
                        self.wait_tile(dve, i + u, 2 + t)
                        dve.wait_ge(silu_ok, i * 2 + (t + 1))
                        dst = A[:, bass.ds(i * 2 + (self.HID + t), 1), :].rearrange("p a n -> p (a n)")
                        nc.vector.tensor_tensor(dst, ps[:, 2 + t, :], g[t], ALU.mult).then_inc(used, 1)
                        dve.sem_inc(ring.bank_free[t], 1)
                        dve.drain().then_inc(ring.bank_free[2 + t], 1)


def second_layer(k, t, l, v_first):
    k.make_schedule(t["w_in_2"][l], t["v_down_2"][0], t["proj_a_2"][l], t["proj_b_2"][l],
                    t["w_out_2"][l], t["w_gu_2"][l], t["w_down_2"][l])
    mu = t["mu_shift_2"][l]
    row = lambda v: v.rearrange("(a p) -> a p", a=1)
    params = [("ada_b", 0, [tiled(t["ada_b_2"][l])]), ("norm1", 0, [tiled(t["norm1_g_2"][l])]),
              ("mu", 0, [tiled(mu[0:1536])]),
              ("mu_l0", 0, [row(mu[1536:1664])]), ("mu_l1", 0, [row(mu[1664:1792])]),
              ("mu_l2", 0, [row(mu[1792:1824])])]
    for name, key in (("w0", "w0_2"), ("a0", "a0_2"), ("k_k", "k_k_2"), ("k_a", "k_a_2"), ("lnx_g", "lnx_g_2"),
                      ("lnx_b", "lnx_b_2"), ("pool_scale", "pool_scale_2")):
        params.append((name, 0, [tiled(t[key][l])]))
    params.append(("v0", 0, [tiled(t["v0_2"][0])]))
    params.append(("r_k", 0, [t["r_k_2"][l].rearrange("(j h) n -> j (h n)", h=2)]))
    params.append(("norm2", 0, [tiled(t["norm2_g_2"][l])]))
    k.mu_v = row(t["mu_v_2"][0])
    k.stage_inputs(t["pool_w_2"][l], params, k.small[:, bass.ds(l * 48 + 192, 48)])
    k.stage_prepare(t["w_up_2"][l], t["a_up_2"][l], t["v_up_2"][0], t["g_up_2"][l], v_first)
    k.stage_token_major()
    k.stage_scan()
    k.stage_gates_output()
    k.stage_merge(["branch", "branch_b"], [k.R, k.YB], 4, 36, 44)
    k.stage_w_out(36, gate=lambda m: k.mod[:, 16 + m:17 + m])
    k.stage_gate_up()
    k.stage_ffn_down(["down", "down_last"], 11, k.HID, gate=lambda m: k.mod[:, 40 + m:41 + m])
    k.core.clear_ring()


def program(nc, t, const_dram, out, rope_scratch, v_first_scratch):
    ctx = ExitStack()
    with ctx:
        first = First(nc, ctx, const_dram)
        stage_prologue(first, t["x"], t["positions"], t["c_2"], const_dram, rope_scratch, v_first_scratch)
        with nc.Fori(0, DEPTH) as l:
            first_layer(first, t, l, rope_scratch)
        first.stage_norm("gain", params=[("gain", 0, [tiled(t["norm_final"])])])
        second = Second(first)
        with nc.Fori(0, DEPTH) as l:
            second_layer(second, t, l, v_first_scratch)
        second.stage_norm("gain", params=[("gain", 0, [tiled(t["final_g_2"])])])
        stage_output(second, out)


def tiled(v, p=P):
    return v.rearrange("(c p) -> c p", p=p)


def first_layer(k, t, l, rope_scratch):
    k.make_schedule(t["w_in"][l], t["w_branch"][l], t["w_out"][l], t["ffn_up"][l], t["ffn_down"][l])
    params = [("norm_mix", 0, [tiled(t["norm_mix"][l])]),
              ("mconv_w", 0, [t["mlstm_conv_w"][l].rearrange("k (c p) -> (k c) p", p=P)]),
              ("mconv_b", 0, [tiled(t["mlstm_conv_b"][l])]),
              ("mlstm_norm", 0, [tiled(t["mlstm_norm"][l])]),
              ("rconv_w", 0, [t["rglru_conv_w"][l].rearrange("k (c p) -> (k c) p", p=P)]),
              ("rconv_b", 0, [tiled(t["rglru_conv_b"][l])]),
              ("lru_ba", 0, [tiled(t["rglru_b_a"][l])]),
              ("lru_bx", 0, [tiled(t["rglru_b_x"][l])]),
              ("lambda", 0, [tiled(t["rglru_lambda"][l])]),
              ("norm_ffn", 0, [tiled(t["norm_ffn"][l])]),
              ("fconv_w", 1, [t["ffn_conv_w"][l].rearrange("k (c p) -> (k c) p", p=P)]),
              ("fconv_b", 1, [tiled(t["ffn_conv_b"][l])])]
    k.stage_attention_inputs(rope_scratch, params)
    k.stage_branch_inputs()
    k.stage_mlstm_lru(t["mlstm_i_bias"][l].rearrange("(h a) -> h a", a=1),
                      t["mlstm_f_bias"][l].rearrange("(h a) -> h a", a=1),
                      t["rglru_w_a"][l], t["rglru_w_x"][l])
    k.stage_gates_attention()
    k.stage_merge(["branch"], [k.YA, k.YB, k.YC], k.GATES, 8, k.T)
    k.stage_w_out(8)
    k.stage_ffn_up(t["ada_w_2"][l], k.small[:, bass.ds(l * 48 + 192, 48)])
    k.stage_ffn_down(["down"], 12, k.HID)
    k.core.clear_ring()


def stage_prologue(k, x_dram, pos_dram, c_dram, const_dram, rope_scratch, v_first_scratch):
    nc, core, ps, A = k.nc, k.core, k.ps, k.arena
    const_in, x_in, x_t, x_ok = core.sem("const_in"), core.sem("x_in"), core.sem("x_t"), core.sem("x_ok")
    ang, sin_ok, table_out, zero_ok = core.sem("angles"), core.sem("sines"), core.sem("table_out"), core.sem("zero")
    table_ok, c_t = core.sem("table_ok"), core.sem("condition_t")
    xt = A[:, 0:8, :].rearrange("p (t k) n -> p t (k n)", t=ST)
    pos_i = A[:, 8, :].bitcast(mybir.dt.int32)
    a0, red, kq, cosr, over = (A[:, 9 + j, :] for j in range(5))
    table = A[:, 14:16, :]
    zero = A[:, 16:20, :]
    TWO_PI = 2 * math.pi
    C1 = 6.28125
    C2 = float(np.float32(np.round((TWO_PI - C1) * 2 ** 20) / 2 ** 20))
    C3 = float(np.float32(TWO_PI - C1 - C2))
    MAGIC = float(1.5 * 2 ** 23)
    PI_DOWN = float(np.nextafter(np.float32(math.pi), np.float32(0)))
    with core.stage() as block:
        @block.sync
        def _(sp):
            sp.dma_start(k.const[:, :], const_dram).then_inc(const_in, 16)
            sp.dma_start(xt, x_dram[0].rearrange("(t p) d -> p t d", p=P)).then_inc(x_in, 16)
            sp.dma_start(A[0:8, 20, 0:P], tiled(c_dram[0])).then_inc(x_in, 16)
            sp.dma_start(pos_i, pos_dram[0:1, :].broadcast_to([P, S])).then_inc(x_in, 16)
            sp.wait_ge(table_ok, 1)
            sp.dma_start(rope_scratch, table).then_inc(table_out, 16)
            sp.wait_ge(zero_ok, 1)
            sp.dma_start(v_first_scratch, zero).then_inc(table_out, 16)
            sp.wait_ge(table_out, 32)

        @block.tensor
        def _(pe):
            pe.wait_ge(const_in, 16)
            pe.wait_ge(x_in, 48)
            nc.tensor.transpose(ps[:, 4, 0:8], A[0:8, 20, 0:P], k.c("ident")[0:8, 0:8]).then_inc(c_t, 1)
            for j in range(KD):
                if j >= 4:
                    pe.wait_ge(x_ok, j - 3)
                for tt in range(ST):
                    last = nc.tensor.transpose(ps[:, j % 4, tt * P:tt * P + P], xt[:, tt, j * P:j * P + P],
                                               k.c("ident"))
                last.then_inc(x_t, 1)

        @block.scalar
        def _(act):
            for j in range(KD):
                act.wait_ge(x_t, j + 1)
                nc.scalar.activation(k.x[:, j, :], ps[:, j % 4, :], ACT.Copy).then_inc(x_ok, 1)
            act.wait_ge(c_t, 1)
            nc.scalar.activation(k.small[:, 184:192], ps[:, 4, 0:8], ACT.Silu)
            act.wait_ge(ang, 1)
            nc.scalar.activation(table[:, 0, :], cosr, ACT.Sin).then_inc(sin_ok, 1)
            nc.scalar.activation(red, red, ACT.Sin).then_inc(sin_ok, 1)

        @block.vector
        def _(dve):
            ts_, tt_, stt_ = nc.vector.tensor_scalar, nc.vector.tensor_tensor, nc.vector.scalar_tensor_tensor
            nc.vector.memset(zero, 0.0)
            nc.vector.memset(k.small[:, 299:300], 0.0)
            dve.drain().then_inc(zero_ok, 1)
            dve.wait_ge(const_in, 16)
            dve.wait_ge(x_in, 48)
            nc.vector.tensor_copy(a0, pos_i)
            dve.drain()
            ts_(a0, a0, k.c("freq"), None, ALU.mult)
            dve.drain()
            ts_(kq, a0, 1.0 / TWO_PI, MAGIC, ALU.mult, ALU.add)
            dve.drain()
            ts_(kq, kq, MAGIC, None, ALU.subtract)
            dve.drain()
            stt_(red, kq, -C1, a0, ALU.mult, ALU.add)
            for c in (C2, C3):
                dve.drain()
                stt_(red, kq, -c, red, ALU.mult, ALU.add)
            dve.drain()
            ts_(cosr, red, math.pi / 2, None, ALU.add)
            dve.drain()
            ts_(over, cosr, math.pi, -TWO_PI, ALU.is_gt, ALU.mult)
            dve.drain()
            tt_(cosr, cosr, over, ALU.add)
            dve.drain()
            ts_(cosr, cosr, PI_DOWN, -PI_DOWN, ALU.min, ALU.max)
            ts_(red, red, PI_DOWN, -PI_DOWN, ALU.min, ALU.max)
            dve.drain().then_inc(ang, 1)
            dve.wait_ge(sin_ok, 2)
            ts_(table[:, 1, :], red, k.c("rope_sign"), None, ALU.mult).then_inc(table_ok, 1)


def stage_output(k, out):
    nc, core, ps, A = k.nc, k.core, k.ps, k.arena
    x_t, y_ok, out_done = core.sem("x_t"), core.sem("y_ok"), core.sem("out_done")
    y = A[:, 0:8, :].rearrange("p (t k) n -> p t (k n)", t=ST)
    with core.stage() as block:
        @block.tensor
        def _(pe):
            for n in range(2 * ST):
                tt, half = divmod(n, 2)
                if n >= 4:
                    pe.wait_ge(y_ok, n - 3)
                for j in range(4):
                    last = nc.tensor.transpose(ps[:, n % 4, j * P:j * P + P],
                                               k.x[:, half * 4 + j, tt * P:tt * P + P], k.c("ident"))
                last.then_inc(x_t, 1)

        @block.scalar
        def _(act):
            for n in range(2 * ST):
                tt, half = divmod(n, 2)
                act.wait_ge(x_t, n + 1)
                nc.scalar.activation(y[:, tt, half * 512:half * 512 + 512], ps[:, n % 4, :], ACT.Copy)\
                    .then_inc(y_ok, 1)

        @block.sync
        def _(sp):
            for tt in range(ST):
                sp.wait_ge(y_ok, 2 * tt + 2)
                sp.dma_start(out[0, tt * P:tt * P + P, :], y[:, tt, :]).then_inc(out_done, 16)
            sp.wait_ge(out_done, 16 * ST)


NAMES = ["x", "positions", "norm_mix", "w_in", "mlstm_conv_w", "mlstm_conv_b", "mlstm_i_bias", "mlstm_f_bias",
         "mlstm_norm", "rglru_conv_w", "rglru_conv_b", "rglru_w_a", "rglru_b_a", "rglru_w_x", "rglru_b_x",
         "rglru_lambda", "w_branch", "w_out", "norm_ffn", "ffn_up", "ffn_conv_w", "ffn_conv_b", "ffn_down",
         "norm_final", "c_2", "ada_w_2", "ada_b_2", "norm1_g_2", "w_in_2", "v_down_2", "mu_shift_2", "mu_v_2",
         "w0_2", "w_up_2", "a0_2", "a_up_2", "v0_2", "v_up_2", "g_up_2", "k_k_2", "k_a_2", "r_k_2", "lnx_g_2",
         "lnx_b_2", "pool_w_2", "pool_scale_2", "proj_a_2", "proj_b_2", "w_out_2", "norm2_g_2", "w_gu_2",
         "w_down_2", "final_g_2"]


def kernel(**inputs):
    import concourse.bacc as _bacc
    from concourse.bass_utils import run_bass_kernel_spmd as _run

    nc = _bacc.Bacc("TRN2", target_bir_lowering=False, num_devices=1)
    arrays, t = {}, {}
    for name in NAMES:
        a = np.ascontiguousarray(inputs[name])
        arrays[f"in_{name}"] = a
        t[name] = nc.dram_tensor(f"in_{name}", a.shape, mybir.dt.from_np(a.dtype), kind="ExternalInput").ap()
    arrays["in_constants"] = constants()
    const_dram = nc.dram_tensor("in_constants", arrays["in_constants"].shape, FP32, kind="ExternalInput").ap()
    out = nc.dram_tensor("out", (1, S, D), FP32, kind="ExternalOutput").ap()
    rope_scratch = nc.dram_tensor("rope_table", (P, 2, S), FP32, kind="Internal").ap()
    v_first_scratch = nc.dram_tensor("v_first", (P, 4, S), FP32, kind="Internal").ap()
    program(nc, t, const_dram, out, rope_scratch, v_first_scratch)
    r = _run(nc, [arrays], core_ids=[0])
    return r.results[0]["out"]
```
